# Optimizing a Trainium2 kernel written in Bass

```python
import jax, jax.numpy as jnp
from jax import lax
import numpy as np

D_MODEL = 1024
BATCH = 1
SEQ = 256
DEPTH = 2

N_META = 16
N_A_LAYERS = DEPTH // 2
N_B_LAYERS = DEPTH - N_A_LAYERS
M_HEADS = 4
M_DV = D_MODEL // M_HEADS
M_DK = M_DV // 2
M_CHUNK = 64
GATE_CAP = 15.0
M_PROJ = 2 * M_HEADS * M_DK + 2 * D_MODEL + 2 * M_HEADS
F_HEADS = 16
F_HD = D_MODEL // F_HEADS
Q_BLOCK = 128
N_GROUPS = 4
EXP_PER_GROUP = 4
N_EXPERTS = N_GROUPS * EXP_PER_GROUP
TOP_K_IN_GROUP = 2
D_EXPERT = D_MODEL // 4
EPS = 1e-6
NEG = -1e30

kernel_name = "mlstm_fox_yoco_hmoe_trunk"

def rmsnorm(x, g):
    xf = x.astype(jnp.float32)
    y = xf * lax.rsqrt(jnp.mean(xf * xf, axis=-1, keepdims=True) + EPS)
    return (y * g.astype(jnp.float32)).astype(x.dtype)

def _heads(t, n, d):
    b, l = t.shape[:2]
    return t.reshape(b, l, n, d).transpose(0, 2, 1, 3)

def mlstm_mixer(h, w_in, b_gate, g_out, w_out):
    B, L, _ = h.shape
    f32 = jnp.float32
    qk_w = M_HEADS * M_DK
    proj = h @ w_in
    q, k, v, o, gates = jnp.split(proj, [qk_w, 2 * qk_w, 2 * qk_w + D_MODEL, 2 * qk_w + 2 * D_MODEL], axis=-1)
    gates = gates.astype(f32) + b_gate.astype(f32)
    gates = GATE_CAP * jnp.tanh(gates / GATE_CAP)
    i_pre = gates[..., :M_HEADS].transpose(0, 2, 1)
    log_f = jax.nn.log_sigmoid(gates[..., M_HEADS:]).transpose(0, 2, 1)
    pad = M_CHUNK - N_META
    def pad_seq(t, val=0.0):
        return jnp.pad(t, [(0, 0), (0, 0), (pad, 0)] + [(0, 0)] * (t.ndim - 3), constant_values=val)
    q = pad_seq(_heads(q, M_HEADS, M_DK).astype(f32) * (M_DK ** -0.5))
    k = pad_seq(_heads(k, M_HEADS, M_DK).astype(f32))
    v = pad_seq(_heads(v, M_HEADS, M_DV).astype(f32))
    li = pad_seq(i_pre, NEG)
    lf = pad_seq(log_f, 0.0)
    Lp = L + pad
    NC = Lp // M_CHUNK
    def chunk(t):
        return t.reshape(t.shape[:2] + (NC, M_CHUNK) + t.shape[3:])
    q, k, v, li, lf = chunk(q), chunk(k), chunk(v), chunk(li), chunk(lf)
    b = jnp.cumsum(lf, axis=-1)
    g_tot = b[..., -1]
    a = g_tot[..., None] - b + li
    m_loc = jnp.max(a, axis=-1)
    wts = jnp.exp(a - m_loc[..., None])
    kv_loc = jnp.einsum('bhncd,bhnce->bhnde', k * wts[..., None], v)
    n_loc = jnp.einsum('bhncd,bhnc->bhnd', k, wts)

    def step(carry, inp):
        c_prev, n_prev, m_prev = carry
        g, m_l, kv_l, n_l = inp
        m_new = jnp.maximum(g + m_prev, m_l)
        s_old = jnp.exp(g + m_prev - m_new)
        s_loc = jnp.exp(m_l - m_new)
        c_new = s_old[..., None, None] * c_prev + s_loc[..., None, None] * kv_l
        n_new = s_old[..., None] * n_prev + s_loc[..., None] * n_l
        return (c_new, n_new, m_new), (c_prev, n_prev, m_prev)

    init = (jnp.zeros((B, M_HEADS, M_DK, M_DV), f32), jnp.zeros((B, M_HEADS, M_DK), f32),
            jnp.zeros((B, M_HEADS), f32))
    mv = lambda t: jnp.moveaxis(t, 2, 0)
    _, (c_st, n_st, m_st) = lax.scan(step, init, (mv(g_tot), mv(m_loc), mv(kv_loc), mv(n_loc)))
    c_st = jnp.moveaxis(c_st, 0, 2)
    n_st = jnp.moveaxis(n_st, 0, 2)
    m_st = jnp.moveaxis(m_st, 0, 2)
    causal = jnp.tril(jnp.ones((M_CHUNK, M_CHUNK), bool))
    dmat = jnp.where(causal, b[..., :, None] - b[..., None, :] + li[..., None, :], NEG)
    bq = b + m_st[..., None]
    m_t = jnp.maximum(jnp.max(dmat, axis=-1), bq)
    s_mat = jnp.einsum('bhncd,bhnsd->bhncs', q, k) * jnp.exp(dmat - m_t[..., None])
    inter = jnp.exp(bq - m_t)
    num = (jnp.einsum('bhncs,bhnse->bhnce', s_mat, v)
           + inter[..., None] * jnp.einsum('bhncd,bhnde->bhnce', q, c_st))
    den = s_mat.sum(-1) + inter * jnp.einsum('bhncd,bhnd->bhnc', q, n_st)
    hout = num / jnp.maximum(jnp.abs(den), jnp.exp(-m_t))[..., None]
    hout = hout.reshape(B, M_HEADS, Lp, M_DV)[:, :, pad:].transpose(0, 2, 1, 3)
    hout = rmsnorm(hout.astype(h.dtype), g_out)
    hout = hout * jax.nn.sigmoid(o.astype(f32)).astype(h.dtype).reshape(B, L, M_HEADS, M_DV)
    return hout.reshape(B, L, D_MODEL) @ w_out

def shared_kv(s, g_kv, w_kv, b_fg, g_k):
    h = rmsnorm(s, g_kv)
    k, v, f_pre = jnp.split(h @ w_kv, [D_MODEL, 2 * D_MODEL], axis=-1)
    k = rmsnorm(_heads(k, F_HEADS, F_HD), g_k)
    v = _heads(v, F_HEADS, F_HD)
    log_f = jax.nn.log_sigmoid(f_pre.astype(jnp.float32) + b_fg.astype(jnp.float32))
    F = jnp.cumsum(log_f, axis=1).transpose(0, 2, 1)
    return k, v, F

def fox_mixer(h, w_q, g_q, w_o, k, v, F):
    B, S, _ = h.shape
    L = k.shape[2]
    q = rmsnorm(_heads(h @ w_q, F_HEADS, F_HD), g_q) * (F_HD ** -0.5)
    nb = S // Q_BLOCK
    qb = q.reshape(B, F_HEADS, nb, Q_BLOCK, F_HD).transpose(2, 0, 1, 3, 4)
    fqb = F[:, :, N_META:].reshape(B, F_HEADS, nb, Q_BLOCK).transpose(2, 0, 1, 3)
    qpos = (N_META + jnp.arange(S, dtype=jnp.int32)).reshape(nb, Q_BLOCK)
    kpos = jnp.arange(L, dtype=jnp.int32)

    def block(args):
        qi, fi, pi = args
        s = (jnp.einsum('bhqd,bhkd->bhqk', qi, k).astype(jnp.float32)
             + fi[..., None] - F[:, :, None, :])
        s = jnp.where(kpos[None, :] <= pi[:, None], s, NEG)
        p = jax.nn.softmax(s, axis=-1).astype(v.dtype)
        return jnp.einsum('bhqk,bhkd->bhqd', p, v)

    o = lax.map(block, (qb, fqb, qpos))
    o = o.transpose(1, 0, 3, 2, 4).reshape(B, S, D_MODEL)
    return o @ w_o

def hier_moe(h, w_group, b_group, w_router, b_router, w_gate, w_up, w_down):
    shp = h.shape
    x = h.reshape(-1, D_MODEL)
    T = x.shape[0]
    f32 = jnp.float32
    gl = (x @ w_group).astype(f32) + b_group.astype(f32)
    top_g = jnp.argmax(gl, axis=-1)
    p_g = jnp.take_along_axis(jax.nn.softmax(gl, axis=-1), top_g[:, None], axis=-1)
    el = ((x @ w_router).astype(f32) + b_router.astype(f32)).reshape(T, N_GROUPS, EXP_PER_GROUP)
    el_g = jnp.take_along_axis(el, top_g[:, None, None], axis=1)[:, 0]
    top_v, top_i = lax.top_k(el_g, TOP_K_IN_GROUP)
    p_e = jax.nn.softmax(top_v, axis=-1) * p_g
    eidx = top_g[:, None] * EXP_PER_GROUP + top_i
    gates = (jax.nn.one_hot(eidx, N_EXPERTS, dtype=f32) * p_e[..., None]).sum(1).astype(x.dtype)
    y = jnp.zeros_like(x)
    for grp in range(N_GROUPS):
        sl = slice(grp * EXP_PER_GROUP, (grp + 1) * EXP_PER_GROUP)
        hg = jnp.einsum('td,edf->tef', x, w_gate[sl])
        hu = jnp.einsum('td,edf->tef', x, w_up[sl])
        act = jax.nn.silu(hg) * hu * gates[:, sl, None]
        y = y + jnp.einsum('tef,efd->td', act, w_down[sl])
    return y.reshape(shp)

def setup_inputs(seed: int = 0) -> dict:
    key = jax.random.key(seed)
    ks = jax.random.split(key, 24)
    f32 = jnp.float32
    def nrm(k, shape, fan):
        return jax.random.normal(k, shape, f32) * (fan ** -0.5)
    def gain(k, shape):
        return 1.0 + 0.02 * jax.random.normal(k, shape, f32)
    NA, NB = N_A_LAYERS, N_B_LAYERS
    kb1, kb2 = jax.random.split(ks[4])
    m_b_gate = jnp.concatenate([
        -2.0 + 0.5 * jax.random.normal(kb1, (NA, M_HEADS), f32),
        jax.random.uniform(kb2, (NA, M_HEADS), f32, 3.0, 6.0)], axis=-1)
    return {
        "x": jax.random.normal(ks[0], (BATCH, SEQ, D_MODEL), f32),
        "meta_tokens": jax.random.normal(ks[1], (N_META, D_MODEL), f32),
        "norm_mix": gain(ks[2], (DEPTH, D_MODEL)),
        "norm_ffn": gain(ks[3], (DEPTH, D_MODEL)),
        "m_w_in": nrm(ks[5], (NA, D_MODEL, M_PROJ), D_MODEL),
        "m_b_gate": m_b_gate,
        "m_g_out": gain(ks[6], (NA, M_HEADS, M_DV)),
        "m_w_out": nrm(ks[7], (NA, D_MODEL, D_MODEL), D_MODEL),
        "kv_norm": gain(ks[8], (D_MODEL,)),
        "kv_w": nrm(ks[9], (D_MODEL, 2 * D_MODEL + F_HEADS), D_MODEL),
        "kv_b_f": jax.random.uniform(ks[10], (F_HEADS,), f32, 1.0, 6.0),
        "k_norm": gain(ks[11], (F_HD,)),
        "f_w_q": nrm(ks[12], (NB, D_MODEL, D_MODEL), D_MODEL),
        "f_q_norm": gain(ks[13], (NB, F_HD)),
        "f_w_o": nrm(ks[14], (NB, D_MODEL, D_MODEL), D_MODEL),
        "moe_w_group": nrm(ks[15], (DEPTH, D_MODEL, N_GROUPS), D_MODEL),
        "moe_b_group": 0.01 * jax.random.normal(ks[16], (DEPTH, N_GROUPS), f32),
        "moe_w_router": nrm(ks[17], (DEPTH, D_MODEL, N_EXPERTS), D_MODEL),
        "moe_b_router": 0.01 * jax.random.normal(ks[18], (DEPTH, N_EXPERTS), f32),
        "moe_w_gate": nrm(ks[19], (DEPTH, N_EXPERTS, D_MODEL, D_EXPERT), D_MODEL),
        "moe_w_up": nrm(ks[20], (DEPTH, N_EXPERTS, D_MODEL, D_EXPERT), D_MODEL),
        "moe_w_down": nrm(ks[21], (DEPTH, N_EXPERTS, D_EXPERT, D_MODEL), D_EXPERT),
    }

def reference(x, meta_tokens, norm_mix, norm_ffn, m_w_in, m_b_gate, m_g_out, m_w_out,
              kv_norm, kv_w, kv_b_f, k_norm, f_w_q, f_q_norm, f_w_o,
              moe_w_group, moe_b_group, moe_w_router, moe_b_router,
              moe_w_gate, moe_w_up, moe_w_down):
    B = x.shape[0]
    meta = jnp.broadcast_to(meta_tokens[None].astype(x.dtype), (B, N_META, D_MODEL))
    h = jnp.concatenate([meta, x], axis=1)
    k_sh = v_sh = F_sh = None
    for l in range(DEPTH):
        if l < N_A_LAYERS:
            h = h + mlstm_mixer(rmsnorm(h, norm_mix[l]), m_w_in[l], m_b_gate[l], m_g_out[l], m_w_out[l])
        else:
            if l == N_A_LAYERS:
                k_sh, v_sh, F_sh = shared_kv(h, kv_norm, kv_w, kv_b_f, k_norm)
                h = h[:, N_META:]
            j = l - N_A_LAYERS
            h = h + fox_mixer(rmsnorm(h, norm_mix[l]), f_w_q[j], f_q_norm[j], f_w_o[j], k_sh, v_sh, F_sh)
        h = h + hier_moe(rmsnorm(h, norm_ffn[l]), moe_w_group[l], moe_b_group[l], moe_w_router[l],
                         moe_b_router[l], moe_w_gate[l], moe_w_up[l], moe_w_down[l])
    return h


_drawn_inputs = setup_inputs


def setup_inputs(seed=0):
    import zlib

    import numpy as np

    out = dict(_drawn_inputs(seed))
    spreads = {}
    factors = {'kv_norm': 5.565, 'k_norm': 4.201, 'f_q_norm': 7.382}
    for name, (base, spread) in spreads.items():
        noise = np.random.default_rng([zlib.crc32(name.encode()), seed]).standard_normal(out[name].shape)
        drawn = base * np.exp(spread * noise) if base else spread * noise
        out[name] = __import__('jax').numpy.asarray(drawn.astype(out[name].dtype))
    for name, factor in factors.items():
        out[name] = (out[name] * factor).astype(out[name].dtype)
    return out
```

```python
import concourse.bass as bass
from concourse import mybir
from contextlib import ExitStack

F32 = mybir.dt.float32
BF16 = mybir.dt.bfloat16
I32 = mybir.dt.int32
ALU = mybir.AluOpType
ACT = mybir.ActivationFunctionType
AX = mybir.AxisListType

P = 128
D = 1024
KB = D // P
SEQ = 256
META = 16
NT = SEQ + META
EPS = 1e-6
NEG = -1e30
TILES = [(0, 128, META), (1, 128, META + 128), (2, META, 0)]
MH, MDK, MDV = 4, 128, 256
GATE_CAP = 15.0
FH, FHD = 16, 64
NE, NG, EPG = 16, 4, 4
FE = 256
CAP = 64
OVF = (NT + CAP - 1) // CAP - 1
SEG = (OVF + 1) * CAP
XROWS = 2 * NT + SEG
UC = 256
RING = 12
EU = 3
GRP = RING // EU


def build(nc, io, out):
    ctx = ExitStack()
    with ctx:
        def sb(name, shape, dt=F32):
            return ctx.enter_context(nc.sbuf_tensor(name, shape, dt))

        sems = {}

        def sem(name):
            if name not in sems:
                sems[name] = ctx.enter_context(nc.semaphore(name))
            return sems[name]

        ring = [sb(f"ring{i}", [P, KB * UC]) for i in range(RING)]
        h = sb("h", [P, 3, D])
        xr = sb("xr", [P, 3, D])
        xT = sb("xT", [P, KB, NT])
        qk_area = sb("qk_area", [P, 2, KB * NT])
        qT = qk_area[:, 0, :].rearrange("p (j t) -> p j t", t=NT)
        kT = qk_area[:, 1, :].rearrange("p (j t) -> p j t", t=NT)
        xg = [qk_area[0:CAP, 0, 0:D], qk_area[0:CAP, 0, D:2 * D]]
        ye = [qk_area[0:CAP, 1, 0:D], qk_area[0:CAP, 1, D:2 * D]]
        gate_area = sb("gate_area", [P, FH * NT])
        sgoT = gate_area[:, 0:KB * NT].rearrange("p (j t) -> p j t", t=NT)
        cspB = gate_area[:, :].rearrange("p (h t) -> p h t", t=NT)
        xgT = [gate_area[:, i * 512:(i + 1) * 512].rearrange("p (k s) -> p k s", s=CAP) for i in (0, 1)]
        yT2 = [gate_area[:, 1024 + i * 512:1536 + i * 512].rearrange("p (k s) -> p k s", s=CAP) for i in (0, 1)]
        sg = [gate_area[:, 2048 + i * 128:2176 + i * 128] for i in (0, 1)]
        actT = [gate_area[:, 2304 + i * 128:2432 + i * 128].rearrange("p (j s) -> p j s", s=CAP) for i in (0, 1)]
        WL = NT + SEQ + 128
        wexp = sb("wexp", [P, MH, WL])
        scb = [wexp[:, 0, i * NT:(i + 1) * NT] for i in (0, 1)]
        prb = [wexp[:, 1, i * NT:(i + 1) * NT] for i in (0, 1)]
        ptb = [wexp[:, 2 + i, 0:3 * 128].rearrange("p (t c) -> p t c", t=3) for i in (0, 1)]
        big = sb("big", [P, 6 * D])
        hn = big[:, 0:3 * D].rearrange("p (t d) -> p t d", t=3)
        xqT = big[:, 0:KB * SEQ].rearrange("p (j t) -> p j t", t=SEQ)
        v0 = big[:, 3 * D:6 * D].rearrange("p (t h e) -> p t h e", t=3, h=MH)
        v1 = big[:, 3 * D:6 * D].rearrange("p (t d) -> p t d", t=3)
        gat = big[:, :].rearrange("p (t c d) -> p t c d", t=3, c=2)
        ox = big[0:CAP, 0:D]
        oy = big[0:CAP, D:2 * D]
        oxT = big[:, 2 * D:2 * D + 512].rearrange("p (k s) -> p k s", s=CAP)
        oyT = big[:, 2 * D + 512:3 * D].rearrange("p (k s) -> p k s", s=CAP)
        osg = big[:, 3 * D:3 * D + 128]
        oact = big[:, 3 * D + 128:3 * D + 256].rearrange("p (j s) -> p j s", s=CAP)
        colT = [sb(f"colT{i}", [P, NT]) for i in (0, 1)]
        sq = [wexp[:, 2 + i, 384:384 + NT] for i in (0, 1)]

        ident = sb("ident", [P, P])
        identb = sb("identb", [P, P], BF16)
        mask_st = big[:, 512:512 + NT]
        negsel = big[0:MH, 0:512].rearrange("p (h c) -> p h c", h=MH)
        mask_ts = sb("mask_ts", [P, P], BF16)
        upper = sb("upper", [P, P], BF16)
        onesb = sb("onesb", [P, P], BF16)
        pair_ones = sb("pair_ones", [P, P])
        onescol = sb("onescol", [P, 1])
        ones16 = sb("ones16", [P, NE])
        eps_col = sb("eps_col", [P, 1])
        scratch_i = sb("scratch_i", [P, NE], I32)
        rev = sb("rev", [P, EPG])
        gains = sb("gains", [P, 5, KB])
        g_out = sb("g_out", [P, KB])
        gk = sb("gk", [P, 1])
        gq = sb("gq", [P, 1])
        w_gates = sb("w_gates", [P, KB, 2 * MH])
        b_gates = sb("b_gates", [P, 2 * MH])
        w_f = sb("w_f", [P, KB, FH])
        b_f = sb("b_f", [P, FH])
        w_rt = sb("w_rt", [P, 2, KB, NG + NE])
        b_rt = sb("b_rt", [P, 2, NG + NE])
        ss = sb("ss", [P, 3])
        rs = sb("rs", [P, 3])
        zg = sb("zg", [P, 3, FH])
        zg2 = sb("zg2", [P, 3, FH])
        zg3 = sb("zg3", [P, 3, FH])
        xr_flat = xr[:, :, :].rearrange("p t d -> p (t d)")
        row_li, row_sp, row_csp, row_c, row_M, row_m, onesrow = [
            xr_flat[0:n_, D + i * NT:D + (i + 1) * NT] for i, n_ in enumerate((MH, FH, FH, MH, MH, MH, FH))]
        tok_cm = sb("tok_cm", [P, 2, 3, MH])
        stile = xr[:, 0, 0:WL]
        den = sb("den", [P, 3, MH])
        den2 = sb("den2", [P, 3, MH])
        ssn = sb("ssn", [P, 3, MH])
        sums = sb("sums", [P, 2, FH])
        rsums = sb("rsums", [P, 2, FH])
        nmax = sb("nmax", [P, 2, FH])
        lg = sb("lg", [P, 3, NG + NE])
        gm = sb("gm", [P, 3, 1])
        t4 = sb("t4", [P, 3, 4])
        t4b = sb("t4b", [P, 3, 4])
        og = sb("og", [P, 3, NG])
        elg = sb("elg", [P, 3, EPG])
        o12 = sb("o12", [P, 2, 3, EPG])
        v12 = sb("v12", [P, 2, 3, 1])
        pg = sb("pg", [P, 3, 1])
        ex = sb("ex", [P, 3, 1])
        dn = sb("dn", [P, 3, 1])
        pe12 = sb("pe12", [P, 2, 3, 1])
        t16 = sb("t16", [P, 3, NE])
        e12 = sb("e12", [P, 2, 3, NE])
        eall = sb("eall", [P, 3, NE], BF16)
        cum = sb("cum", [P, NE])
        cnt = sb("cnt", [P, NE])
        slots = sb("slots", [P, 3, NE])
        idxf = sb("idxf", [P, 2, 3])
        idx = sb("idx", [P, 2, 3], I32)
        TBL_CNT, TBL_OVF = NE + GRP, 2 * NE + GRP
        tbl = sb("tbl", [1, TBL_OVF + NE], I32)
        novf = sb("novf", [1, NE])
        novf_sum = sb("novf_sum", [1, NE])

        bank = [ctx.enter_context(nc.psum_tensor(f"bank{i}", [P, 512], F32)) for i in range(8)]
        xs = [nc.dram_tensor(f"xs{l}", [XROWS, D], F32, kind="Internal").ap() for l in (0, 1)]
        ys = [nc.dram_tensor(f"ys{l}", [XROWS, D], F32, kind="Internal").ap() for l in (0, 1)]
        cs_dram = nc.dram_tensor("cs_dram", [FH, NT], F32, kind="Internal").ap()

        PH = {"q0": 8, "k0": 8 // 2, "v0": 8, "o0": 8, "out0": 8, "k1": 8, "v1": 8, "q1": 8, "out1": 8}
        PH["q0"] = PH["k0"] = 4
        PHASES = ["q0", "k0", "v0", "o0", "out0", "k1", "v1", "q1", "out1"]
        U_FIRST, u = {}, 0
        for ph in PHASES:
            if ph == "k1":
                u += NE * EU
            U_FIRST[ph] = u
            u += PH[ph] // 2
        U_MOE = [U_FIRST["out0"] + 4, U_FIRST["out1"] + 4]

        def cols(w, c0):
            return w[:, c0:c0 + UC]

        w_in, kv_w = io["m_w_in"][0], io["kv_w"]
        SRC = {"q0": (w_in, 0, "(p k) c -> p k c"), "k0": (w_in, 512, "(p k) c -> p k c"),
               "v0": (w_in, 1024, "(p k) c -> p k c"), "o0": (w_in, 2048, "(p k) c -> p k c"),
               "out0": (io["m_w_out"][0], 0, "(k p) c -> p k c"), "k1": (kv_w, 0, "(p k) c -> p k c"),
               "v1": (kv_w, D, "(p k) c -> p k c"), "q1": (io["f_w_q"][0], 0, "(p k) c -> p k c"),
               "out1": (io["f_w_o"][0], 0, "(k p) c -> p k c")}

        def unit(s):
            return ring[s % RING][:, :].rearrange("p (k c) -> p k c", c=UC)

        def unit_down(s):
            return ring[s % RING][:, :].rearrange("p (j d) -> p j d", d=D)

        def arrived(s):
            return sem(f"unit_arrived{s % RING}")

        TR = ["norm0", "vt0", "ht0", "add0", "ffn0", "norm1", "vt1", "ht1", "add1", "ffn1"]
        ORDER = {"proj": PHASES, "tr": TR}

        def before(kind, ph):
            return sum(PH.get(p, 8) for p in ORDER[kind][:ORDER[kind].index(ph)])

        def done(kind, ph, n):
            return sem(f"{kind}_done"), before(kind, ph) + n

        def read(kind, ph, b, n):
            return sem(f"{kind}_read{b}"), before(kind, ph) // 2 + n

        def wait_bank(pe, kind, ph, j):
            if before(kind, ph) + j >= 2:
                pe.wait_ge(*read(kind, ph, j % 2, j // 2))

        def alone(eng):
            eng.sem_inc(sem("wait_holder"), 1)

        block = ctx.enter_context(nc.Block())

        @block.sync
        def _(sp):
            def projection_is_through(old):
                for ph in PHASES:
                    if U_FIRST[ph] <= old < U_FIRST[ph] + PH[ph] // 2:
                        sp.wait_ge(*done("proj", ph, 2 * (old - U_FIRST[ph] + 1)))

            def load_units(ph):
                w, c0, lay = SRC[ph]
                for i in range(PH[ph] // 2):
                    s = U_FIRST[ph] + i
                    old = s - RING
                    projection_is_through(old)
                    if U_MOE[0] <= old < U_FIRST["k1"]:
                        e, part = divmod(old - U_MOE[0], EU)
                        sp.wait_ge(sem("down_done0"), e + 1 if part == 2 else max(e, 1))
                    sp.dma_start(unit(s), cols(w, c0 + i * UC).rearrange(lay, k=KB)).then_inc(arrived(s), 16)

            def load_expert(l, e, s):
                sp.dma_start(unit(s), io["moe_w_gate"][l, e, :, :].rearrange("(p k) c -> p k c", k=KB)) \
                    .then_inc(arrived(s), 16)
                sp.dma_start(unit(s + 1), io["moe_w_up"][l, e, :, :].rearrange("(p k) c -> p k c", k=KB)) \
                    .then_inc(arrived(s + 1), 16)

            def load_down(l, e, s):
                sp.dma_start(unit_down(s + 2), io["moe_w_down"][l, e, :, :].rearrange("(j p) d -> p j d", p=P)) \
                    .then_inc(arrived(s + 2), 16)

            def load_moe(l):
                base = U_MOE[l]
                for e in range(GRP):
                    for part in range(EU):
                        projection_is_through(base + EU * e + part - RING)
                        if part == 1:
                            load_expert(l, e, base + EU * e)
                        if part == 2:
                            load_down(l, e, base + EU * e)
                with sp.Fori(1, NE // GRP) as g:
                    for j in range(GRP):
                        if j == 0:
                            sp.wait_ge(sem(f"down_done{l}"), GRP * (g - 1) + 1)
                        else:
                            sp.wait_ge(sem(f"down_done{l}"), GRP * (g - 1) + j)
                        load_expert(l, GRP * g + j, base + EU * j)
                        sp.wait_ge(sem(f"down_done{l}"), GRP * (g - 1) + j + 1)
                        load_down(l, GRP * g + j, base + EU * j)

            for ph in PHASES[:5]:
                load_units(ph)
            load_moe(0)
            for ph in PHASES[5:]:
                load_units(ph)
            load_moe(1)
            for t in (0, 1):
                sp.wait_ge(sem("result_ready"), t + 1)
                sp.dma_start(out[0, t * P:(t + 1) * P, :], h[:, t, :]).then_inc(sem("out_written"), 16)
            sp.wait_ge(sem("out_written"), 32)

        @block.gpsimd
        def _(pool):
            pool.memset(ident[:, :], 0.0).then_inc(sem("pool_c"), 1)
            pool.memset(mask_st[:, :], 0.0).then_inc(sem("pool_c"), 1)
            pool.memset(mask_ts[:, :], 0.0).then_inc(sem("pool_c"), 1)
            pool.memset(upper[:, :], 1.0).then_inc(sem("pool_c"), 1)
            pool.memset(negsel[:, :, :], 0.0).then_inc(sem("pool_c"), 1)
            pool.memset(pair_ones[:, :], 1.0).then_inc(sem("pool_c"), 1)
            pool.wait_ge(sem("pool_c"), 6)
            pool.affine_select(out=ident[:, :], in_=ident[:, :], compare_op=ALU.not_equal, fill=1.0, base=0,
                               pattern=[[-1, P]], channel_multiplier=1).then_inc(sem("ident_ready"), 1)
            pool.affine_select(out=pair_ones[:, 0:64], in_=pair_ones[:, 0:64], compare_op=ALU.is_ge, fill=0.0,
                               base=63, pattern=[[0, 64]], channel_multiplier=-1).then_inc(sem("pool_c"), 1)
            pool.affine_select(out=pair_ones[:, 64:P], in_=pair_ones[:, 64:P], compare_op=ALU.is_ge, fill=0.0,
                               base=-64, pattern=[[0, 64]], channel_multiplier=1).then_inc(sem("pool_c"), 1)
            pool.affine_select(out=mask_st[:, :], in_=mask_st[:, :], compare_op=ALU.is_ge, fill=NEG, base=0,
                               pattern=[[1, NT]], channel_multiplier=-1).then_inc(sem("pool_c"), 1)
            pool.affine_select(out=mask_ts[:, :], in_=mask_ts[:, :], compare_op=ALU.is_ge, fill=NEG, base=0,
                               pattern=[[-1, P]], channel_multiplier=1).then_inc(sem("pool_c"), 1)
            pool.affine_select(out=upper[:, :], in_=upper[:, :], compare_op=ALU.is_gt, fill=0.0, base=0,
                               pattern=[[1, P]], channel_multiplier=-1).then_inc(sem("pool_c"), 1)
            pool.affine_select(out=negsel[:, :, :], in_=negsel[:, :, :], compare_op=ALU.not_equal, fill=-1.0,
                               base=0, pattern=[[-1, MH], [0, P]], channel_multiplier=1).then_inc(sem("pool_c"), 1)
            pool.memset(onesb[:, :], 1.0).then_inc(sem("pool_c"), 1)
            pool.memset(onescol[:, :], 1.0).then_inc(sem("pool_c"), 1)
            pool.wait_ge(sem("pool_c"), 14)
            pool.iota(scratch_i[:, 0:EPG], pattern=[[-1, EPG]], base=EPG, channel_multiplier=0) \
                .then_inc(sem("pool_c"), 1)
            pool.wait_ge(sem("pool_c"), 15)
            pool.tensor_copy(rev[:, :], scratch_i[:, 0:EPG]).then_inc(sem("consts_ready"), 1)
            for l, nt in ((0, NT), (1, SEQ)):
                for rows in (xs[l], ys[l]):
                    pool.dma_start(rows[2 * nt:2 * nt + CAP, :], io["x"][0, 0:CAP, :]).then_inc(sem("slack_written"), 16)

            def moe(l):
                tiles = TILES[:3 - l]
                nscat = 2 * len(tiles)
                pool.wait_ge(sem(f"idx_ready{l}"), 1)
                for t, rows, _ in tiles:
                    for c in (0, 1):
                        pool.indirect_dma_start(
                            out=xs[l], out_offset=bass.IndirectOffsetOnAxis(ap=idx[0:rows, c, t:t + 1], axis=0),
                            in_=xr[0:rows, t, :], in_offset=None).then_inc(sem(f"scattered{l}"), 16)
                pool.wait_ge(sem("slack_written"), 64)
                pool.wait_ge(sem(f"scattered{l}"), 16 * nscat)
                pool.wait_ge(sem(f"tbl_ready{l}"), 1)

                def load_x(b, e):
                    first = pool.value_load(tbl[0:1, bass.ds(e, 1)], min_val=0, max_val=2 * NT)
                    pool.dma_start(xg[b], xs[l][bass.ds(first, CAP), :]).then_inc(sem(f"x_in{l}_{b}"), 16)

                def overflow(i):
                    n = pool.value_load(tbl[0:1, bass.ds(TBL_CNT + i, 1)], min_val=0, max_val=NT)
                    with pool.If(n > CAP):
                        before_i = pool.value_load(tbl[0:1, bass.ds(TBL_OVF + i, 1)], min_val=0, max_val=NE * OVF)
                        with pool.Fori(1, OVF + 1) as tt:
                            k = before_i + tt
                            with pool.If(n > CAP * tt):
                                first = pool.value_load(tbl[0:1, bass.ds(i, 1)], min_val=0, max_val=2 * NT)
                                pool.dma_start(ox, xs[l][bass.ds(first + CAP * tt, CAP), :]) \
                                    .then_inc(sem(f"ox_in{l}"), 16)
                                pool.wait_ge(sem(f"ovf_dve{l}"), 5 * k)
                                alone(pool)
                                pool.dma_start(ys[l][bass.ds(first + CAP * tt, CAP), :], oy) \
                                    .then_inc(sem(f"oy_written{l}"), 16)
                                pool.wait_ge(sem(f"oy_written{l}"), 16 * k)
                                alone(pool)

                def write_y(b, e, v, before):
                    if before is not None:
                        pool.wait_ge(sem(f"y_written{l}_{1 - b}"), before)
                    pool.wait_ge(sem(f"y_act{l}"), v)
                    pool.wait_ge(sem(f"y_dve{l}"), v)
                    first = pool.value_load(tbl[0:1, bass.ds(e, 1)], min_val=0, max_val=2 * NT)
                    pool.dma_start(ys[l][bass.ds(first, CAP), :], ye[b]).then_inc(sem(f"y_written{l}_{b}"), 16)

                load_x(0, 0)
                load_x(1, 1)
                pool.wait_ge(sem(f"tx_done{l}"), 1)
                load_x(0, 2)

                def turn(i, s):
                    pool.wait_ge(sem(f"tx_done{l}"), i + 2)
                    load_x((s + 1) % 2, i + 3)
                    overflow(i)

                for i in range(GRP):
                    turn(i, i)
                    if i >= 2:
                        write_y(i % 2, i - 2, i - 1, 16 * ((i - 1) // 2) if i > 2 else None)
                with pool.Fori(1, NE // GRP) as g:
                    for s in range(GRP):
                        turn(GRP * g + s, s)
                        write_y(s % 2, GRP * g + s - 2, GRP * g + s - 1, 32 * g + 16 * ((s - 1) // 2))
                for i in (NE, NE + 1):
                    write_y(i % 2, i - 2, i - 1, 16 * ((i - 1) // 2))
                for b in (0, 1):
                    pool.wait_ge(sem(f"y_written{l}_{b}"), 16 * NE // 2)
                for t, rows, _ in tiles:
                    for c in (0, 1):
                        pool.indirect_dma_start(
                            out=gat[0:rows, t, c, :], out_offset=None, in_=ys[l][0:2 * NT + CAP if l == 0 else 2 * SEQ + CAP, :],
                            in_offset=bass.IndirectOffsetOnAxis(ap=idx[0:rows, c, t:t + 1], axis=0)) \
                            .then_inc(sem(f"gathered{l}_{t}"), 16)
                for b, n in ((0, 10), (1, 9)):
                    pool.wait_ge(sem(f"x_in{l}_{b}"), 16 * n)

            moe(0)
            pool.wait_ge(sem("csp1_ready"), 1)
            pool.dma_start(cs_dram, row_csp[:, :]).then_inc(sem("cs_out"), 16)
            pool.wait_ge(sem("cs_out"), 16)
            pool.dma_start(cspB, cs_dram.partition_broadcast(P)).then_inc(sem("cspB_ready"), 16)
            moe(1)

        @block.scalar
        def _(act):
            chain = [0]

            def link(ins):
                chain[0] += 1
                ins.then_inc(sem("act_chain"), 1)
                act.wait_ge(sem("act_chain"), chain[0])

            act.dma_start(h[:, 0:2, :], io["x"][0].rearrange("(t p) d -> p t d", p=P)).then_inc(sem("x_loaded"), 16)
            act.dma_start(h[0:META, 2, :], io["meta_tokens"]).then_inc(sem("x_loaded"), 16)
            with nc.allow_non_contiguous_dma(reason="small parameter vectors"):
                for i, g in enumerate((io["norm_mix"][0], io["norm_ffn"][0], io["kv_norm"], io["norm_mix"][1],
                                       io["norm_ffn"][1])):
                    act.dma_start(gains[:, i, :], g.rearrange("(p k) -> p k", k=KB)).then_inc(sem("small_loaded"), 16)
                act.dma_start(w_gates[:, :, :], w_in[:, 3072:3080].rearrange("(p k) c -> p k c", k=KB)) \
                    .then_inc(sem("small_loaded"), 16)
                act.dma_start(b_gates[:, :], io["m_b_gate"][0].partition_broadcast(P)) \
                    .then_inc(sem("small_loaded"), 16)
                act.dma_start(g_out[:, :], io["m_g_out"][0].rearrange("h (j p) -> p (h j)", p=P)) \
                    .then_inc(sem("small2_loaded"), 16)
                for half in (0, 1):
                    act.dma_start(gk[64 * half:64 * half + 64, :], io["k_norm"].rearrange("(p o) -> p o", o=1)) \
                        .then_inc(sem("small2_loaded"), 16)
                    act.dma_start(gq[64 * half:64 * half + 64, :], io["f_q_norm"][0].rearrange("(p o) -> p o", o=1)) \
                        .then_inc(sem("small2_loaded"), 16)
                act.dma_start(w_f[:, :, :], kv_w[:, 2 * D:2 * D + FH].rearrange("(p k) c -> p k c", k=KB)) \
                    .then_inc(sem("small2_loaded"), 16)
                act.dma_start(b_f[:, :], io["kv_b_f"].partition_broadcast(P)).then_inc(sem("small2_loaded"), 16)
                for l in (0, 1):
                    act.dma_start(w_rt[:, l, :, 0:NG], io["moe_w_group"][l].rearrange("(p k) c -> p k c", k=KB)) \
                        .then_inc(sem("small2_loaded"), 16)
                    act.dma_start(w_rt[:, l, :, NG:NG + NE], io["moe_w_router"][l].rearrange("(p k) c -> p k c", k=KB)) \
                        .then_inc(sem("small2_loaded"), 16)
                    act.dma_start(b_rt[:, l, 0:NG], io["moe_b_group"][l].partition_broadcast(P)) \
                        .then_inc(sem("small2_loaded"), 16)
                    act.dma_start(b_rt[:, l, NG:NG + NE], io["moe_b_router"][l].partition_broadcast(P)) \
                        .then_inc(sem("small2_loaded"), 16)

            def inverse_rms(name, tiles):
                for t, rows, _ in tiles:
                    ins = act.activation(gate_area[0:rows, t * D:(t + 1) * D], h[0:rows, t, :], ACT.Square,
                                         accum_out=ss[0:rows, t:t + 1])
                link(ins)
                link(act.activation(rs[:, :], ss[:, :], ACT.Ln, bias=eps_col[:, :], scale=1.0 / D))
                act.activation(rs[:, :], rs[:, :], ACT.Exp, scale=-0.5).then_inc(sem(f"rs_{name}"), 1)

            def norm_evac(ph, g, n=NT):
                for j in range(1, KB, 2):
                    act.wait_ge(*done("tr", ph, j + 1))
                    act.activation(xT[:, j, 0:n], bank[3][:, 0:n], ACT.Copy, scale=gains[:, g, j:j + 1]) \
                        .then_inc(sem("tr_read1"), 1)

            act.wait_ge(sem("x_loaded"), 32)
            act.wait_ge(sem("init_ready"), 1)
            inverse_rms("norm0", TILES)
            act.wait_ge(sem("small_loaded"), 16 * 7)
            norm_evac("norm0", 0)
            act.wait_ge(sem("gate_z"), 1)
            act.activation(zg2[:, :, 0:8], zg[:, :, 0:8], ACT.Exp, scale=2.0 / GATE_CAP).then_inc(sem("gate_e"), 1)
            act.wait_ge(sem("gate_g"), 1)
            link(act.activation(zg2[:, :, 4:8], zg[:, :, 4:8], ACT.Exp, scale=-1.0))
            act.activation(zg[:, :, 4:8], zg2[:, :, 4:8], ACT.Ln, bias=1.0).then_inc(sem("gate_sp"), 1)
            for j in range(PH["q0"]):
                act.wait_ge(*done("proj", "q0", j + 1))
                act.activation(qT[:, j, :], bank[j % 2][:, 0:NT], ACT.Copy, scale=MDK ** -0.5) \
                    .then_inc(sem(f"proj_read{j % 2}"), 1)
            act.wait_ge(sem("cm_tok"), 1)
            act.activation(tok_cm[:, 1, :, :], tok_cm[:, 1, :, :], ACT.Exp, scale=-1.0).then_inc(sem("expm_ready"), 1)
            for hd in range(MH):
                act.wait_ge(sem("warg"), hd + 1)
                link(act.activation(wexp[0:META, hd, 0:NT], wexp[0:META, hd, 0:NT], ACT.Exp))
                act.activation(wexp[:, hd, NT:WL], wexp[:, hd, NT:WL], ACT.Exp).then_inc(sem("wexp_ready"), 1)

            def pt_evac(u):
                act.wait_ge(sem("pt_done"), u + 1)
                if u >= 2:
                    act.wait_ge(sem("pv_done"), u - 1)
                src = bank[7][:, 0:384].rearrange("p (t c) -> p t c", t=3)
                act.activation(ptb[1][:, 0:2, :], src[:, 0:2, :], ACT.Copy)
                act.activation(ptb[1][0:META, 2, :], src[0:META, 2, :], ACT.Copy).then_inc(sem("pt_read1"), 1)

            def v_evac(l, dst2):
                for j in range(8):
                    act.wait_ge(*done("tr", f"vt{l}", j + 1))
                    src = bank[2 + j % 2][:, 0:384].rearrange("p (t c) -> p t c", t=3)
                    act.activation(dst2(j, slice(0, P), slice(0, 2)), src[:, 0:2, :], ACT.Copy)
                    act.activation(dst2(j, slice(0, META), 2), src[0:META, 2, :], ACT.Copy) \
                        .then_inc(sem(f"tr_read{j % 2}"), 1)

            v_evac(0, lambda j, p, t: v0[p, t, j // 2, (j % 2) * P:(j % 2) * P + P])
            for j in range(8):
                act.wait_ge(*done("proj", "o0", j + 1))
                act.activation(sgoT[:, j, :], bank[j % 2][:, 0:NT], ACT.Sigmoid) \
                    .then_inc(sem(f"proj_read{j % 2}"), 1)
            for hd in range(MH):
                act.wait_ge(sem("num_done"), hd + 1)
                for t, rows, _ in TILES:
                    ins = act.activation(hn[0:rows, t, hd * MDV:(hd + 1) * MDV], bank[(0, 1, 2)[t]][0:rows, 0:MDV],
                                         ACT.Copy)
                ins.then_inc(sem("num_read_act"), 1)
                act.wait_ge(sem("num_read_act"), hd + 1)
                for t, rows, _ in TILES:
                    dump = (colT[0][:, 0:MDV], colT[1][:, 0:MDV], xr_flat[0:META, 2 * D:2 * D + MDV])[t]
                    ins = act.activation(dump, hn[0:rows, t, hd * MDV:(hd + 1) * MDV], ACT.Square,
                                         accum_out=ssn[0:rows, t, hd:hd + 1])
                ins.then_inc(sem("ssn_ready"), 1)
            act.wait_ge(sem("den2_ready"), 1)
            link(act.activation(ssn[:, :, :], den2[:, :, :], ACT.Ln))
            act.activation(ssn[:, :, :], ssn[:, :, :], ACT.Exp, scale=-0.5).then_inc(sem("hscale"), 1)

            def out_evac(l, n):
                for j in range(8):
                    act.wait_ge(*done("proj", f"out{l}", j + 1))
                    if j >= 2:
                        act.wait_ge(*done("tr", f"add{l}", j - 1))
                    act.activation(colT[j % 2][:, 0:n], bank[j % 2][:, 0:n], ACT.Copy) \
                        .then_inc(sem(f"proj_read{j % 2}"), 1)

            out_evac(0, NT)

            def moe(l):
                tiles = TILES[:3 - l]
                for b in (0, 1):
                    act.wait_ge(*read("tr", f"add{l}", b, 4))
                inverse_rms(f"ffn{l}", tiles)
                norm_evac(f"ffn{l}", 1 if l == 0 else 4, NT if l == 0 else SEQ)
                act.wait_ge(sem(f"gl_sub{l}"), 1)
                act.activation(t4b[:, :, :], t4[:, :, :], ACT.Exp).then_inc(sem(f"gl_exp{l}"), 1)
                act.wait_ge(sem(f"v_sub{l}"), 1)
                act.activation(ex[:, :, :], dn[:, :, :], ACT.Exp).then_inc(sem(f"v_exp{l}"), 1)
                act.wait_ge(sem(f"tbl_ready{l}"), 1)

                def overflow(i):
                    n = act.value_load(tbl[0:1, bass.ds(TBL_CNT + i, 1)], min_val=0, max_val=NT)
                    with act.If(n > CAP):
                        before_i = act.value_load(tbl[0:1, bass.ds(TBL_OVF + i, 1)], min_val=0, max_val=NE * OVF)
                        with act.Fori(1, OVF + 1) as tt:
                            k = before_i + tt
                            with act.If(n > CAP * tt):
                                act.wait_ge(sem(f"ovf_pe{l}"), 5 * k - 3)
                                act.activation(osg, bank[7][:, 0:128], ACT.Silu).then_inc(sem(f"ovf_act{l}"), 1)
                                act.wait_ge(sem(f"ovf_act{l}"), k)
                                alone(act)

                def turn(i, s, experts=True, yt=True, yrow=True, wait_buf=True):
                    if experts:
                        act.wait_ge(sem(f"gu_done{l}"), i + 1)
                        act.activation(sg[s % 2], bank[1 + s % 2][:, 0:128], ACT.Silu) \
                            .then_inc(sem(f"silu_done{l}"), 1)
                        overflow(i)
                    if yt:
                        act.wait_ge(sem(f"down_done{l}"), i)
                        act.activation(yT2[(s + 1) % 2], bank[3 + (s + 1) % 2][:, :].rearrange(
                            "p (k s) -> p k s", s=CAP), ACT.Copy).then_inc(sem(f"yT_read{l}"), 1)
                    if yrow:
                        if wait_buf:
                            act.wait_ge(sem(f"y_written{l}_{s % 2}"), 8 * (i - s) + 16 * (s // 2) - 16)
                        act.wait_ge(sem(f"ty_done{l}"), i - 1)
                        act.activation(ye[s % 2][:, 0:512], bank[5][0:CAP, :], ACT.Copy) \
                            .then_inc(sem(f"y_act{l}"), 1)

                for i in range(GRP):
                    turn(i, i, yt=i >= 1, yrow=i >= 2, wait_buf=False)
                with act.Fori(1, NE // GRP) as g:
                    for s in range(GRP):
                        turn(GRP * g + s, s)
                turn(NE, 0, experts=False)
                turn(NE + 1, 1, experts=False, yt=False)

            moe(0)
            act.wait_ge(sem("combined0"), 3)
            inverse_rms("norm1", TILES)
            for j in range(1, KB, 2):
                act.wait_ge(*done("tr", "norm1", j + 1))
                act.activation(xT[:, j, :], bank[3][:, 0:NT], ACT.Copy, scale=gains[:, 2, j:j + 1])
                act.activation(xqT[:, j, :], bank[3][:, META:NT], ACT.Copy, scale=gains[:, 3, j:j + 1]) \
                    .then_inc(sem("tr_read1"), 1)
            act.wait_ge(sem("f_abs"), 1)
            link(act.activation(zg2[:, :, :], zg2[:, :, :], ACT.Exp, scale=-1.0))
            act.activation(zg2[:, :, :], zg2[:, :, :], ACT.Ln, bias=1.0).then_inc(sem("f_ln"), 1)

            def head_norm(ph, n):
                for j in range(8):
                    act.wait_ge(*done("proj", ph, j + 1))
                    if j >= 2:
                        act.wait_ge(sem(f"hn_done_{ph}"), j - 1)
                    act.activation(colT[j % 2][:, 0:n], bank[j % 2][:, 0:n], ACT.Copy)
                    act.activation(sq[j % 2][:, 0:n], bank[j % 2][:, 0:n], ACT.Square) \
                        .then_inc(sem(f"proj_read{j % 2}"), 1)
                    act.wait_ge(sem(f"ssq_done_{ph}"), j + 1)
                    link(act.activation(sq[j % 2][:, 0:n], bank[4 + j % 2][:, 0:n], ACT.Ln, bias=eps_col[:, :],
                                        scale=1.0 / FHD))
                    act.activation(sq[j % 2][:, 0:n], sq[j % 2][:, 0:n], ACT.Exp, scale=-0.5) \
                        .then_inc(sem(f"rstd_{ph}"), 1)

            head_norm("k1", NT)
            v_evac(1, lambda j, p, t: v1[p, t, j * P:(j + 1) * P])
            head_norm("q1", SEQ)
            for u in range(2 * FH):
                hd, qt = divmod(u, 2)
                nk = META + P * (qt + 1)
                act.wait_ge(sem("score_ready"), u + 1)
                if u >= 2:
                    act.wait_ge(sem("pt_done"), u - 1)
                act.activation(prb[u % 2][:, 0:nk], scb[u % 2][:, 0:nk], ACT.Exp, scale=-1.0,
                               bias=nmax[:, qt, hd:hd + 1], accum_out=sums[:, qt, hd:hd + 1]) \
                    .then_inc(sem("prob_ready"), 1)
                if qt == 1 and u >= 3:
                    pt_evac(u - 2)
            pt_evac(2 * FH - 1)
            out_evac(1, SEQ)
            moe(1)

        @block.vector
        def _(dve):
            chain = [0]

            def link(ins):
                chain[0] += 1
                ins.then_inc(sem("dve_chain"), 1)
                dve.wait_ge(sem("dve_chain"), chain[0])

            dve.memset(ss[:, :], 1.0)
            dve.memset(rs[:, :], 1.0)
            dve.memset(zg[:, :, :], 0.0)
            dve.memset(zg2[:, :, :], 0.0)
            dve.memset(lg[:, :, :], 0.0)
            dve.memset(slots[:, :, :], 0.0)
            dve.memset(ssn[:, :, :], 1.0)
            dve.memset(den[:, :, :], 1.0)
            dve.memset(tok_cm[:, :, :, :], 0.0)
            dve.memset(tbl[:, :], 0)
            dve.memset(ones16[:, :], 1.0)
            dve.memset(eps_col[:, :], EPS).then_inc(sem("init_ready"), 1)
            dve.wait_ge(sem("init_ready"), 1)

            def scale_rows(name, tiles):
                dve.wait_ge(sem(f"rs_{name}"), 1)
                for t, rows, _ in tiles:
                    dve.tensor_scalar(xr[0:rows, t, :], h[0:rows, t, :], rs[0:rows, t:t + 1], None, ALU.mult) \
                        .then_inc(sem(f"xr_{name}"), 1)

            def norm_evac(ph, g, n=NT):
                for j in range(0, KB, 2):
                    dve.wait_ge(*done("tr", ph, j + 1))
                    dve.tensor_scalar(xT[:, j, 0:n], bank[2][:, 0:n], gains[:, g, j:j + 1], None, ALU.mult) \
                        .then_inc(sem("tr_read0"), 1)

            scale_rows("norm0", TILES)
            dve.wait_ge(sem("small_loaded"), 16 * 7)
            norm_evac("norm0", 0)
            dve.wait_ge(sem("gate_mm"), 1)
            for t, rows, _ in TILES:
                ins = dve.tensor_tensor(zg[0:rows, t, 0:8], bank[4][0:rows, t * 8:t * 8 + 8], b_gates[0:rows, :],
                                        ALU.add)
            ins.then_inc(sem("gate_z"), 1)
            dve.wait_ge(sem("gate_e"), 1)
            link(dve.tensor_scalar(zg2[:, :, 0:8], zg2[:, :, 0:8], 1.0, None, ALU.add))
            link(dve.reciprocal(zg2[:, :, 0:8], zg2[:, :, 0:8]))
            dve.tensor_scalar(zg[:, :, 0:8], zg2[:, :, 0:8], -2 * GATE_CAP, GATE_CAP, ALU.mult, ALU.add) \
                .then_inc(sem("gate_g"), 1)
            dve.wait_ge(sem("gate_rows"), 1)
            dve.memset(onesrow[:, :], 1.0)
            dve.tensor_copy(row_li[:, :], bank[5][0:MH, 0:NT])
            link(dve.tensor_copy(row_sp[0:MH, :], bank[6][0:MH, 0:NT]))
            dve.wait_ge(sem("consts_ready"), 1)
            dve.tensor_copy(identb[:, :], ident[:, :]).then_inc(sem("identb_ready"), 1)
            link(dve.tensor_tensor_scan(row_csp[0:MH, :], onesrow[0:MH, :], row_sp[0:MH, :], 0.0, ALU.mult, ALU.add))
            link(dve.tensor_tensor(row_c[:, :], row_li[:, :], row_csp[0:MH, :], ALU.add))
            link(dve.tensor_tensor_scan(row_M[:, :], row_c[:, :], row_c[:, :], -3.0e38, ALU.max, ALU.max))
            dve.tensor_tensor(row_m[:, :], row_M[:, :], row_csp[0:MH, :], ALU.subtract).then_inc(sem("rows_ready"), 1)
            for j in range(PH["k0"]):
                dve.wait_ge(*done("proj", "k0", j + 1))
                dve.tensor_copy(kT[:, j, :], bank[j % 2][:, 0:NT]).then_inc(sem(f"proj_read{j % 2}"), 1)
            dve.wait_ge(sem("cm_mm"), 1)
            for t, rows, _ in TILES:
                ins = dve.tensor_copy(tok_cm[0:rows, :, t, :],
                                      bank[4][0:rows, t * 8:t * 8 + 8].rearrange("p (a b) -> p a b", a=2))
            ins.then_inc(sem("cm_tok"), 1)
            dve.wait_ge(sem("cm_tok"), 1)
            for hd in range(MH):
                dve.wait_ge(sem("negM_mm"), hd + 1)
                nm = bank[5 + hd % 2]
                dve.scalar_tensor_tensor(wexp[0:META, hd, 0:NT], nm[0:META, 0:NT], tok_cm[0:META, 0, 2, hd:hd + 1],
                                         mask_st[0:META, :], ALU.add, ALU.add)
                dve.scalar_tensor_tensor(wexp[:, hd, NT:NT + SEQ], nm[:, META:NT], tok_cm[:, 0, 0, hd:hd + 1],
                                         mask_st[:, 0:SEQ], ALU.add, ALU.add)
                dve.scalar_tensor_tensor(wexp[:, hd, NT + SEQ:WL], nm[:, META + P:NT], tok_cm[:, 0, 1, hd:hd + 1],
                                         mask_st[:, 0:P], ALU.add, ALU.add).then_inc(sem("warg"), 1)

            def col_evac(l, n):
                for j in range(8):
                    dve.wait_ge(*done("proj", f"v{l}", j + 1))
                    if j >= 2:
                        dve.wait_ge(*done("tr", f"vt{l}", j - 1))
                    dve.tensor_copy(colT[j % 2][:, 0:n], bank[j % 2][:, 0:n]).then_inc(sem(f"proj_read{j % 2}"), 1)

            def pt_evac(u):
                dve.wait_ge(sem("pt_done"), u + 1)
                if u >= 2:
                    dve.wait_ge(sem("pv_done"), u - 1)
                src = bank[6][:, 0:384].rearrange("p (t c) -> p t c", t=3)
                dve.tensor_copy(ptb[0][:, 0, :], src[:, 0, :])
                dve.tensor_copy(ptb[0][0:META, 2, :], src[0:META, 2, :]).then_inc(sem("pt_read0"), 1)

            col_evac(0, NT)
            for hd in range(MH):
                dve.wait_ge(sem("wexp_ready"), hd + 1)
                dve.wait_ge(sem("s_done"), hd + 1)
                if hd:
                    dve.wait_ge(sem("num_done"), hd)
                dve.tensor_tensor(stile[0:META, 0:NT], bank[4][0:META, 0:NT], wexp[0:META, hd, 0:NT], ALU.mult)
                dve.tensor_tensor(stile[:, NT:WL], bank[5][:, 0:WL - NT], wexp[:, hd, NT:WL], ALU.mult) \
                    .then_inc(sem("st_ready"), 1)
                dve.wait_ge(sem("num_done"), hd + 1)
                dve.wait_ge(sem("num_read_act"), hd + 1)
                for t, rows, _ in TILES:
                    ins = dve.tensor_copy(den[0:rows, t, hd:hd + 1], bank[t][0:rows, MDV:MDV + 1])
                ins.then_inc(sem("num_read"), 1)
            dve.wait_ge(sem("num_read"), MH)
            dve.wait_ge(sem("expm_ready"), 1)
            dve.wait_ge(sem("ssn_ready"), MH)
            link(dve.scalar_tensor_tensor(den2[:, :, :], den[:, :, :], -1.0, den[:, :, :], ALU.mult, ALU.max))
            link(dve.tensor_tensor(den2[:, :, :], den2[:, :, :], tok_cm[:, 1, :, :], ALU.max))
            link(dve.tensor_tensor(den2[:, :, :], den2[:, :, :], den2[:, :, :], ALU.mult))
            link(dve.tensor_scalar(den2[:, :, :], den2[:, :, :], EPS, None, ALU.mult))
            dve.scalar_tensor_tensor(den2[:, :, :], ssn[:, :, :], 1.0 / MDV, den2[:, :, :], ALU.mult, ALU.add) \
                .then_inc(sem("den2_ready"), 1)
            dve.wait_ge(sem("hscale"), 1)
            for t, rows, _ in TILES:
                for hd in range(MH):
                    c = slice(hd * MDV, (hd + 1) * MDV)
                    ins = dve.tensor_scalar(hn[0:rows, t, c], hn[0:rows, t, c], ssn[0:rows, t, hd:hd + 1], None,
                                            ALU.mult)
                ins.then_inc(sem("hn_ready"), 1)
            dve.wait_ge(sem("small2_loaded"), 16 * 15)
            for j in range(8):
                dve.wait_ge(*done("tr", "ht0", j + 1))
                dve.scalar_tensor_tensor(xT[:, j, :], bank[2 + j % 2][:, 0:NT], g_out[:, j:j + 1], sgoT[:, j, :],
                                         ALU.mult, ALU.mult).then_inc(sem(f"tr_read{j % 2}"), 1)

            def add_evac(l):
                for j in range(8):
                    dve.wait_ge(*done("tr", f"add{l}", j + 1))
                    src = bank[2 + j % 2][:, 0:384].rearrange("p (t c) -> p t c", t=3)
                    c = slice(j * P, (j + 1) * P)
                    if l == 0:
                        dve.tensor_tensor(h[0:META, 2, c], h[0:META, 2, c], src[0:META, 2, :], ALU.add)
                    ins = dve.tensor_tensor(h[:, 0:2, c], h[:, 0:2, c], src[:, 0:2, :], ALU.add)
                    ins.then_inc(sem(f"tr_read{j % 2}"), 1)
                dve.wait_ge(*read("tr", f"add{l}", 0, 4))
                dve.wait_ge(*read("tr", f"add{l}", 1, 4))

            add_evac(0)

            def route(l):
                tiles = TILES[:3 - l]
                scale_rows(f"ffn{l}", tiles)
                norm_evac(f"ffn{l}", 1 if l == 0 else 4, NT if l == 0 else SEQ)
                dve.wait_ge(sem(f"router_mm{l}"), 1)
                for t, rows, _ in tiles:
                    ins = dve.tensor_tensor(lg[0:rows, t, :], bank[4][0:rows, t * 20:t * 20 + 20], b_rt[0:rows, l, :],
                                            ALU.add)
                link(ins)
                bc3 = [P, 3, 4]
                revb = rev[:, :].unsqueeze(1).to_broadcast(bc3)

                def first_max(dst, src, mx):
                    link(dve.tensor_tensor(t4[:, :, :], src, mx.to_broadcast(bc3), ALU.is_equal))
                    link(dve.tensor_tensor(t4[:, :, :], t4[:, :, :], revb, ALU.mult))
                    link(dve.tensor_reduce(dn[:, :, :], t4[:, :, :], AX.X, ALU.max))
                    link(dve.tensor_tensor(dst, t4[:, :, :], dn[:, :, :].to_broadcast(bc3), ALU.is_equal))

                gl = lg[:, :, 0:NG]
                link(dve.tensor_reduce(gm[:, :, :], gl, AX.X, ALU.max))
                first_max(og[:, :, :], gl, gm[:, :, :])
                dve.tensor_tensor(t4[:, :, :], gl, gm[:, :, :].to_broadcast(bc3), ALU.subtract) \
                    .then_inc(sem(f"gl_sub{l}"), 1)
                dve.wait_ge(sem(f"gl_exp{l}"), 1)
                link(dve.tensor_reduce(pg[:, :, :], t4b[:, :, :], AX.X, ALU.add))
                link(dve.reciprocal(pg[:, :, :], pg[:, :, :]))
                el = lg[:, :, NG:NG + NE].rearrange("p t (g j) -> p t g j", g=NG)
                t16v = t16[:, :, :].rearrange("p t (g j) -> p t g j", g=NG)
                full = [P, 3, NG, EPG]
                ogb = og[:, :, :].unsqueeze(3).to_broadcast(full)
                link(dve.tensor_tensor(t16v, el, ogb, ALU.mult))
                link(dve.tensor_reduce(elg[:, :, :], t16v.rearrange("p t g j -> p t j g"), AX.X, ALU.add))
                link(dve.tensor_reduce(v12[:, 0, :, :], elg[:, :, :], AX.X, ALU.max))
                first_max(o12[:, 0, :, :], elg[:, :, :], v12[:, 0, :, :])
                link(dve.scalar_tensor_tensor(elg[:, :, :], o12[:, 0, :, :], NEG, elg[:, :, :], ALU.mult, ALU.add))
                link(dve.tensor_reduce(v12[:, 1, :, :], elg[:, :, :], AX.X, ALU.max))
                first_max(o12[:, 1, :, :], elg[:, :, :], v12[:, 1, :, :])
                dve.tensor_tensor(dn[:, :, :], v12[:, 1, :, :], v12[:, 0, :, :], ALU.subtract) \
                    .then_inc(sem(f"v_sub{l}"), 1)
                for c in (0, 1):
                    link(dve.tensor_tensor(e12[:, c, :, :].rearrange("p t (g j) -> p t g j", g=NG), ogb,
                                           o12[:, c, :, :].unsqueeze(2).to_broadcast(full), ALU.mult))
                dve.tensor_tensor(eall[:, :, :], e12[:, 0, :, :], e12[:, 1, :, :], ALU.add) \
                    .then_inc(sem(f"eall_ready{l}"), 1)
                dve.wait_ge(sem(f"v_exp{l}"), 1)
                link(dve.tensor_scalar(dn[:, :, :], ex[:, :, :], 1.0, None, ALU.add))
                link(dve.reciprocal(dn[:, :, :], dn[:, :, :]))
                link(dve.tensor_tensor(pe12[:, 0, :, :], dn[:, :, :], pg[:, :, :], ALU.mult))
                link(dve.tensor_tensor(pe12[:, 1, :, :], pe12[:, 0, :, :], ex[:, :, :], ALU.mult))
                dve.wait_ge(sem(f"pos_mm{l}"), 1)
                link(dve.tensor_copy(cnt[:, :], bank[4][:, 48:64]))
                link(dve.tensor_tensor_scan(cum[:, :], ones16[:, :], cnt[:, :], 0.0, ALU.mult, ALU.add))
                link(dve.tensor_tensor(cum[:, :], cum[:, :], cnt[:, :], ALU.subtract))
                for t, rows, _ in tiles:
                    ins = dve.tensor_tensor(slots[0:rows, t, :], bank[4][0:rows, t * 16:t * 16 + 16], cum[0:rows, :],
                                            ALU.add)
                link(ins)
                for c in (0, 1):
                    link(dve.tensor_tensor(t16[:, :, :], slots[:, :, :], e12[:, c, :, :], ALU.mult))
                    link(dve.tensor_reduce(idxf[:, c, :], t16[:, :, :], AX.X, ALU.add))
                dve.tensor_copy(idx[:, :, :], idxf[:, :, :]).then_inc(sem(f"idx_ready{l}"), 1)
                dve.tensor_copy(tbl[0:1, 0:NE], cum[0:1, :])
                dve.tensor_copy(tbl[0:1, TBL_CNT:TBL_CNT + NE], cnt[0:1, :])
                link(dve.tensor_scalar(novf[:, :], cnt[0:1, :], float(CAP), None, ALU.is_gt))
                for tt in range(2, OVF + 1):
                    link(dve.scalar_tensor_tensor(novf[:, :], cnt[0:1, :], float(CAP * tt), novf[:, :], ALU.is_gt,
                                                  ALU.add))
                link(dve.tensor_tensor_scan(novf_sum[:, :], ones16[0:1, :], novf[:, :], 0.0, ALU.mult, ALU.add))
                dve.tensor_tensor(tbl[0:1, TBL_OVF:TBL_OVF + NE], novf_sum[:, :], novf[:, :], ALU.subtract) \
                    .then_inc(sem(f"tbl_ready{l}"), 1)
                dve.wait_ge(sem(f"tbl_ready{l}"), 1)

            def moe(l):
                route(l)
                tiles = TILES[:3 - l]
                gb = gains[:, 1 if l == 0 else 4, :].unsqueeze(2).to_broadcast([P, KB, CAP])

                def bank_rows(b):
                    return bank[b][:, :].rearrange("p (k s) -> p k s", s=CAP)

                def overflow(i):
                    n = dve.value_load(tbl[0:1, bass.ds(TBL_CNT + i, 1)], min_val=0, max_val=NT)
                    with dve.If(n > CAP):
                        before_i = dve.value_load(tbl[0:1, bass.ds(TBL_OVF + i, 1)], min_val=0, max_val=NE * OVF)
                        with dve.Fori(1, OVF + 1) as tt:
                            k = before_i + tt
                            with dve.If(n > CAP * tt):
                                od, op = sem(f"ovf_dve{l}"), sem(f"ovf_pe{l}")
                                dve.wait_ge(op, 5 * k - 4)
                                dve.tensor_tensor(oxT, bank_rows(7), gb, ALU.mult).then_inc(od, 1)
                                dve.wait_ge(sem(f"ovf_act{l}"), k)
                                dve.tensor_tensor(oact, osg.rearrange("p (j s) -> p j s", s=CAP),
                                                  bank[7][:, 128:256].rearrange("p (j s) -> p j s", s=CAP), ALU.mult) \
                                    .then_inc(od, 1)
                                dve.wait_ge(op, 5 * k - 2)
                                dve.tensor_copy(oyT, bank_rows(7)).then_inc(od, 1)
                                for half in (0, 1):
                                    dve.wait_ge(op, 5 * k - 1 + half)
                                    dve.tensor_copy(oy[:, 512 * half:512 * half + 512], bank[7][0:CAP, :]) \
                                        .then_inc(od, 1)
                                dve.wait_ge(od, 5 * k)
                                alone(dve)

                def x_evac(s, v):
                    dve.wait_ge(sem(f"tx_done{l}"), v)
                    dve.tensor_tensor(xgT[s % 2], bank_rows(0), gb, ALU.mult).then_inc(sem(f"xT_read{l}"), 1)

                def turn(i, s, experts=True, yrow=True, wait_buf=True, wait_act=True):
                    if experts:
                        x_evac(s + 1, i + 2)
                        dve.wait_ge(sem(f"silu_done{l}"), i + 1)
                        if wait_act:
                            dve.wait_ge(sem(f"down_done{l}"), i - 1)
                        dve.tensor_tensor(actT[s % 2], sg[s % 2].rearrange("p (j s) -> p j s", s=CAP),
                                          bank[1 + s % 2][:, 128:256].rearrange("p (j s) -> p j s", s=CAP), ALU.mult) \
                            .then_inc(sem(f"act_ready{l}"), 1)
                        overflow(i)
                    if yrow:
                        if wait_buf:
                            dve.wait_ge(sem(f"y_written{l}_{s % 2}"), 8 * (i - s) + 16 * (s // 2) - 16)
                        dve.wait_ge(sem(f"ty_done{l}"), i - 1)
                        dve.tensor_copy(ye[s % 2][:, 512:1024], bank[6][0:CAP, :]).then_inc(sem(f"y_dve{l}"), 1)

                x_evac(0, 1)
                for i in range(GRP):
                    turn(i, i, yrow=i >= 2, wait_buf=False, wait_act=i >= 2)
                with dve.Fori(1, NE // GRP) as g:
                    for s in range(GRP):
                        turn(GRP * g + s, s)
                turn(NE, 0, experts=False)
                turn(NE + 1, 1, experts=False)
                for t, rows, _ in tiles:
                    dve.wait_ge(sem(f"gathered{l}_{t}"), 32)
                    for c in (0, 1):
                        ins = dve.scalar_tensor_tensor(h[0:rows, t, :], gat[0:rows, t, c, :], pe12[0:rows, c, t, :],
                                                       h[0:rows, t, :], ALU.mult, ALU.add)
                        if c == 0:
                            link(ins)
                    ins.then_inc(sem("combined0" if l == 0 else "result_ready"), 1)

            moe(0)
            dve.wait_ge(sem("combined0"), 3)
            scale_rows("norm1", TILES)
            for j in range(0, KB, 2):
                dve.wait_ge(*done("tr", "norm1", j + 1))
                dve.tensor_scalar(xT[:, j, :], bank[2][:, 0:NT], gains[:, 2, j:j + 1], None, ALU.mult)
                dve.tensor_scalar(xqT[:, j, :], bank[2][:, META:NT], gains[:, 3, j:j + 1], None, ALU.mult) \
                    .then_inc(sem("tr_read0"), 1)
            dve.wait_ge(sem("f_mm"), 1)
            for t, rows, _ in TILES:
                ins = dve.tensor_tensor(zg[0:rows, t, :], bank[4][0:rows, t * FH:(t + 1) * FH], b_f[0:rows, :], ALU.add)
            link(ins)
            dve.scalar_tensor_tensor(zg2[:, :, :], zg[:, :, :], -1.0, zg[:, :, :], ALU.mult, ALU.max) \
                .then_inc(sem("f_abs"), 1)
            link(dve.tensor_scalar(zg3[:, :, :], zg[:, :, :], 0.0, None, ALU.min))
            dve.wait_ge(sem("f_ln"), 1)
            dve.tensor_tensor(zg[:, :, :], zg2[:, :, :], zg3[:, :, :], ALU.subtract).then_inc(sem("f_sp"), 1)
            dve.wait_ge(sem("f_rows"), 1)
            dve.memset(onesrow[:, :], 1.0)
            link(dve.tensor_copy(row_sp[:, :], bank[6][0:FH, 0:NT]))
            dve.tensor_tensor_scan(row_csp[:, :], onesrow[:, :], row_sp[:, :], 0.0, ALU.mult, ALU.add) \
                .then_inc(sem("csp1_ready"), 1)
            dve.tensor_scalar(gq[:, :], gq[:, :], FHD ** -0.5, None, ALU.mult).then_inc(sem("gq_scaled"), 1)
            dve.wait_ge(sem("gq_scaled"), 1)

            def head_norm(ph, dst, g, n):
                for j in range(8):
                    dve.wait_ge(sem(f"rstd_{ph}"), j + 1)
                    dve.scalar_tensor_tensor(dst[:, j, 0:n], colT[j % 2][:, 0:n], g[:, :], sq[j % 2][:, 0:n], ALU.mult,
                                             ALU.mult).then_inc(sem(f"hn_done_{ph}"), 1)

            head_norm("k1", kT, gk, NT)
            dve.wait_ge(sem("hn_done_k1"), 8)
            col_evac(1, NT)
            head_norm("q1", qT, gq, SEQ)
            dve.wait_ge(sem("cspB_ready"), 16)
            for u in range(2 * FH):
                hd, qt = divmod(u, 2)
                nk = META + P * (qt + 1)
                dve.wait_ge(sem("qk_done"), u + 1)
                if u >= 2:
                    dve.wait_ge(sem("prob_ready"), u - 1)
                dve.tensor_tensor_reduce(out=scb[u % 2][:, 0:nk], in0=bank[4 + u % 2][:, 0:nk],
                                         in1=cspB[:, hd, 0:nk], scale=-1.0, scalar=3.0e38, op0=ALU.add, op1=ALU.min,
                                         accum_out=nmax[:, qt, hd:hd + 1]).then_inc(sem("score_ready"), 1)
                if qt == 1 and u >= 3:
                    pt_evac(u - 3)
            pt_evac(2 * FH - 2)
            dve.wait_ge(sem("prob_ready"), 2 * FH)
            link(dve.reciprocal(rsums[:, :, :], sums[:, :, :]))
            dve.wait_ge(sem("pv_done"), 2 * FH)
            for qt in (0, 1):
                for half in (0, 1):
                    ins = dve.tensor_tensor(
                        hn[:, qt, half * 512:half * 512 + 512].rearrange("p (h e) -> p h e", e=FHD),
                        bank[2 * qt + half][:, :].rearrange("p (h e) -> p h e", e=FHD),
                        rsums[:, qt, 8 * half:8 * half + 8].unsqueeze(2).to_broadcast([P, 8, FHD]), ALU.mult)
            ins.then_inc(sem("o_ready"), 1)
            for j in range(8):
                dve.wait_ge(*done("tr", "ht1", j + 1))
                dve.tensor_copy(xT[:, j, 0:SEQ], bank[2 + j % 2][:, 0:SEQ]).then_inc(sem(f"tr_read{j % 2}"), 1)
            add_evac(1)
            moe(1)

        @block.tensor
        def _(pe):
            def project(ph, j, x, n, u_base=None):
                s = U_FIRST[ph] + j // 2
                if j % 2 == 0:
                    pe.wait_ge(arrived(s), 16 * (s // RING + 1))
                wait_bank(pe, "proj", ph, j)
                w = unit(s)
                for k in range(KB):
                    ins = pe.matmul(bank[j % 2][:, 0:n], w[:, k, (j % 2) * P:(j % 2) * P + P], x[:, k, 0:n],
                                    start=(k == 0), stop=(k == KB - 1))
                ins.then_inc(sem("proj_done"), 1)

            def norm_tr(ph, n):
                tiles = TILES if n == NT else TILES[:2]
                off = NT - n
                name = ph
                for t, _, _ in tiles:
                    pe.wait_ge(sem(f"xr_{name}"), t + 1)
                for k in range(KB):
                    wait_bank(pe, "tr", ph, k)
                    for t, rows, c0 in tiles:
                        ins = pe.transpose(bank[2 + k % 2][:, c0 - off:c0 - off + rows], xr[0:rows, t, k:D:KB],
                                           ident[0:rows, 0:rows])
                    ins.then_inc(sem("tr_done"), 1)

            def col_tr(ph, src_ph, j, tiles, off=0):
                pe.wait_ge(*read("proj", src_ph, j % 2, j // 2 + 1))
                wait_bank(pe, "tr", ph, j)
                for t, rows, c0 in tiles:
                    ins = pe.transpose(bank[2 + j % 2][0:rows, t * P:(t + 1) * P], colT[j % 2][:, c0 - off:c0 - off + rows],
                                       ident[:, :])
                ins.then_inc(sem("tr_done"), 1)

            def row_tr(ph, tiles, off=0):
                for j in range(8):
                    wait_bank(pe, "tr", ph, j)
                    for t, rows, c0 in tiles:
                        ins = pe.transpose(bank[2 + j % 2][:, c0 - off:c0 - off + rows], hn[0:rows, t, j * P:(j + 1) * P],
                                           ident[0:rows, 0:rows])
                    ins.then_inc(sem("tr_done"), 1)

            def small_mm(w, width, ready, tiles, off=0):
                for t, rows, c0 in tiles:
                    for k in range(KB):
                        ins = pe.matmul(bank[4][0:rows, t * width:(t + 1) * width],
                                        xT[:, k, c0 - off:c0 - off + rows], w[:, k, :], start=(k == 0),
                                        stop=(k == KB - 1))
                ins.then_inc(sem(ready), 1)

            pe.wait_ge(sem("ident_ready"), 1)
            norm_tr("norm0", NT)
            for b in (0, 1):
                pe.wait_ge(*read("tr", "norm0", b, 4))
            small_mm(w_gates, 8, "gate_mm", TILES)
            for j in range(4):
                project("q0", j, xT, NT)
            pe.wait_ge(sem("gate_sp"), 1)
            for b, c in ((5, 0), (6, 4)):
                for t, rows, c0 in TILES:
                    ins = pe.transpose(bank[b][0:MH, c0:c0 + rows], zg[0:rows, t, c:c + MH], ident[0:rows, 0:rows])
            ins.then_inc(sem("gate_rows"), 1)
            for j in range(4):
                project("k0", j, xT, NT)
            pe.wait_ge(sem("rows_ready"), 1)
            for t, rows, c0 in TILES:
                for a, r in ((0, row_c), (1, row_m)):
                    ins = pe.transpose(bank[4][0:rows, t * 8 + 4 * a:t * 8 + 4 * a + 4], r[:, c0:c0 + rows],
                                       ident[0:MH, 0:MH])
            ins.then_inc(sem("cm_mm"), 1)
            for hd in range(MH):
                if hd >= 2:
                    pe.wait_ge(sem("warg"), hd - 1)
                pe.matmul(bank[5 + hd % 2][:, 0:NT], negsel[:, hd, :], row_M[:, :], start=True, stop=True) \
                    .then_inc(sem("negM_mm"), 1)
            for j in range(9):
                if j < 8:
                    project("v0", j, xT, NT)
                if j >= 1:
                    col_tr("vt0", "v0", j - 1, TILES)
            for j in range(8):
                project("o0", j, xT, NT)
            for b in (0, 1):
                pe.wait_ge(*read("tr", "vt0", b, 4))
            pe.wait_ge(sem("warg"), MH)

            def head_scores(hd):
                if hd == 0:
                    pe.wait_ge(*read("proj", "q0", 1, 2))
                    pe.wait_ge(*read("proj", "k0", 1, 2))
                else:
                    pe.wait_ge(sem("st_ready"), hd)
                pe.matmul(bank[4][0:META, 0:NT], kT[:, hd, 0:META], qT[:, hd, :], start=True, stop=True)
                pe.matmul(bank[5][:, 0:SEQ], kT[:, hd, META:META + P], qT[:, hd, META:NT], start=True, stop=True)
                pe.matmul(bank[5][:, SEQ:SEQ + P], kT[:, hd, META + P:NT], qT[:, hd, META + P:NT], start=True,
                          stop=True).then_inc(sem("s_done"), 1)

            head_scores(0)
            for hd in range(MH):
                pe.wait_ge(sem("st_ready"), hd + 1)
                if hd == 0:
                    for b in (0, 1):
                        pe.wait_ge(*read("proj", "o0", b, 4))
                else:
                    pe.wait_ge(sem("num_read"), hd)
                    pe.wait_ge(sem("num_read_act"), hd)
                srcs = {2: [(0, META, 2)], 0: [(META, META, 2), (NT, P, 0)],
                        1: [(META + P, META, 2), (NT + P, P, 0), (NT + SEQ, P, 1)]}
                for t, rows, _ in TILES:
                    for rhs_cols, rhs in ((slice(0, MDV), None), (slice(MDV, MDV + 1), onescol)):
                        for n_, (c, kr, st) in enumerate(srcs[t]):
                            ins = pe.matmul(bank[t][0:rows, rhs_cols], stile[0:kr, c:c + rows],
                                            v0[0:kr, st, hd, :] if rhs is None else onescol[0:kr, :],
                                            start=(n_ == 0), stop=(n_ == len(srcs[t]) - 1))
                ins.then_inc(sem("num_done"), 1)
                if hd + 1 < MH:
                    head_scores(hd + 1)
            pe.wait_ge(sem("num_read"), MH)
            pe.wait_ge(sem("num_read_act"), MH)
            pe.wait_ge(sem("hn_ready"), 3)
            row_tr("ht0", TILES)
            for b in (0, 1):
                pe.wait_ge(*read("tr", "ht0", b, 4))
            for j in range(9):
                if j < 8:
                    project("out0", j, xT, NT)
                if j >= 1:
                    col_tr("add0", "out0", j - 1, TILES)

            def moe(l):
                tiles = TILES[:3 - l]
                n = NT if l == 0 else SEQ
                off = NT - n
                base = U_MOE[l]
                norm_tr(f"ffn{l}", n)
                for b in (0, 1):
                    pe.wait_ge(*read("tr", f"ffn{l}", b, 4))
                if l == 0:
                    pe.wait_ge(sem("small2_loaded"), 16 * 15)
                small_mm(w_rt[:, l, :, :], NG + NE, f"router_mm{l}", tiles, off)
                pe.wait_ge(sem(f"eall_ready{l}"), 1)
                pe.wait_ge(sem("consts_ready"), 1)
                nt = len(tiles)
                jobs = [(t, rows, [(q, onesb) for q in range(t)] + [(t, upper)]) for t, rows, _ in tiles]
                for t, rows, terms in jobs + [(3, P, [(q, onesb) for q in range(nt)])]:
                    for m, (q, lhs) in enumerate(terms):
                        kr = tiles[q][1]
                        ins = pe.matmul(bank[4][0:rows, t * NE:(t + 1) * NE], lhs[0:kr, 0:rows], eall[0:kr, q, :],
                                        start=(m == 0), stop=(m == len(terms) - 1))
                ins.then_inc(sem(f"pos_mm{l}"), 1)
                pe.wait_ge(sem(f"tbl_ready{l}"), 1)

                def to_cols(b, src):
                    for k in range(KB):
                        ins = pe.transpose(bank[b][:, k * CAP:(k + 1) * CAP], src[:, k:D:KB], ident[0:CAP, 0:CAP])
                    return ins

                def gate_up(b, s, x):
                    for a in (0, 1):
                        w = unit(s + a)
                        for f in (0, 1):
                            for k in range(KB):
                                ins = pe.matmul(bank[b][:, (2 * a + f) * CAP:(2 * a + f + 1) * CAP],
                                                w[:, k, f * P:(f + 1) * P], x[:, k, :], start=(k == 0),
                                                stop=(k == KB - 1))
                    return ins

                def down(b, s, a):
                    w = unit_down(s + 2)
                    for k in range(KB):
                        for f in (0, 1):
                            ins = pe.matmul(bank[b][:, k * CAP:(k + 1) * CAP], w[:, f, k * P:(k + 1) * P], a[:, f, :],
                                            start=(f == 0), stop=(f == 1))
                    return ins

                def to_rows(b, src, half):
                    for k in range(4):
                        ins = pe.transpose(bank[b][0:CAP, k * P:(k + 1) * P], src[:, 4 * half + k, :], ident[:, :])
                    return ins

                def overflow(i, s, turns):
                    n_ = pe.value_load(tbl[0:1, bass.ds(TBL_CNT + i, 1)], min_val=0, max_val=NT)
                    op, od = sem(f"ovf_pe{l}"), sem(f"ovf_dve{l}")
                    with pe.If(n_ > CAP):
                        pe.wait_ge(arrived(s + 2), turns(s + 2))
                        alone(pe)
                        before_i = pe.value_load(tbl[0:1, bass.ds(TBL_OVF + i, 1)], min_val=0, max_val=NE * OVF)
                        with pe.Fori(1, OVF + 1) as tt:
                            k = before_i + tt
                            with pe.If(n_ > CAP * tt):
                                pe.wait_ge(sem(f"ox_in{l}"), 16 * k)
                                alone(pe)
                                to_cols(7, ox).then_inc(op, 1)
                                pe.wait_ge(od, 5 * k - 4)
                                gate_up(7, s, oxT).then_inc(op, 1)
                                pe.wait_ge(od, 5 * k - 3)
                                down(7, s, oact).then_inc(op, 1)
                                for half in (0, 1):
                                    pe.wait_ge(od, 5 * k - 2 + half)
                                    alone(pe)
                                    to_rows(7, oyT, half).then_inc(op, 1)
                                pe.wait_ge(op, 5 * k)
                                alone(pe)

                def turn(i, g, s, experts=True, dn_=True, rows_=True, first=False):
                    def turns(u):
                        return 16 * (g + (u // RING) + 1)

                    if experts:
                        pe.wait_ge(sem(f"xT_read{l}"), i + 1)
                        b = (s + 1) % 2
                        pe.wait_ge(sem(f"x_in{l}_{b}"), 32 * g + 16 * ((s + 1) // 2 + 1))
                        alone(pe)
                        to_cols(0, xg[b]).then_inc(sem(f"tx_done{l}"), 1)
                        u = base + EU * s
                        pe.wait_ge(arrived(u), turns(u))
                        pe.wait_ge(arrived(u + 1), turns(u + 1))
                        if not first or s >= 2:
                            pe.wait_ge(sem(f"act_ready{l}"), i - 1)
                        gate_up(1 + s % 2, u, xgT[s % 2]).then_inc(sem(f"gu_done{l}"), 1)
                        overflow(i, u, turns)
                    if dn_:
                        sp_ = (s - 1) % GRP
                        u = base + EU * sp_
                        tg = turns(u + 2) - (16 if s == 0 else 0)
                        pe.wait_ge(arrived(u + 2), tg)
                        pe.wait_ge(sem(f"act_ready{l}"), i)
                        if not first or s >= 3:
                            pe.wait_ge(sem(f"yT_read{l}"), i - 2)
                        down(3 + (s + 1) % 2, u, actT[(s + 1) % 2]).then_inc(sem(f"down_done{l}"), 1)
                    if rows_:
                        pe.wait_ge(sem(f"yT_read{l}"), i - 1)
                        if not first or s >= 3:
                            pe.wait_ge(sem(f"y_act{l}"), i - 2)
                            pe.wait_ge(sem(f"y_dve{l}"), i - 2)
                        alone(pe)
                        to_rows(5, yT2[s % 2], 0)
                        to_rows(6, yT2[s % 2], 1).then_inc(sem(f"ty_done{l}"), 1)

                pe.wait_ge(sem(f"x_in{l}_0"), 16)
                to_cols(0, xg[0]).then_inc(sem(f"tx_done{l}"), 1)
                for i in range(GRP):
                    turn(i, 0, i, dn_=i >= 1, rows_=i >= 2, first=True)
                with pe.Fori(1, NE // GRP) as g:
                    for s in range(GRP):
                        turn(GRP * g + s, g, s)
                turn(NE, NE // GRP, 0, experts=False)
                turn(NE + 1, NE // GRP, 1, experts=False, dn_=False)
                pe.wait_ge(sem(f"y_act{l}"), NE)
                pe.wait_ge(sem(f"y_dve{l}"), NE)
                pe.wait_ge(sem(f"xT_read{l}"), NE + 1)

            moe(0)
            norm_tr("norm1", NT)
            for b in (0, 1):
                pe.wait_ge(*read("tr", "norm1", b, 4))
            small_mm(w_f, FH, "f_mm", TILES)

            def head_norm(ph, x, n):
                for j in range(9):
                    if j < 8:
                        project(ph, j, x, n)
                    if j >= 1:
                        i = j - 1
                        pe.wait_ge(*read("proj", ph, i % 2, i // 2 + 1))
                        if i >= 2:
                            pe.wait_ge(sem(f"rstd_{ph}"), i - 1)
                        pe.matmul(bank[4 + i % 2][:, 0:n], pair_ones[:, :], sq[i % 2][:, 0:n], start=True, stop=True) \
                            .then_inc(sem(f"ssq_done_{ph}"), 1)
                    if ph == "k1" and j == 0:
                        pe.wait_ge(sem("f_sp"), 1)
                        for t, rows, c0 in TILES:
                            ins = pe.transpose(bank[6][0:FH, c0:c0 + rows], zg[0:rows, t, :], ident[0:rows, 0:rows])
                        ins.then_inc(sem("f_rows"), 1)

            head_norm("k1", xT, NT)
            for j in range(9):
                if j < 8:
                    project("v1", j, xT, NT)
                if j >= 1:
                    col_tr("vt1", "v1", j - 1, TILES)
            pe.wait_ge(sem("rstd_k1"), 8)
            head_norm("q1", xqT, SEQ)
            pe.wait_ge(sem("hn_done_q1"), 8)
            for b in (0, 1):
                pe.wait_ge(*read("tr", "vt1", b, 4))
            NU = 2 * FH

            def qk(u):
                hd, qt = divmod(u, 2)
                nk = META + P * (qt + 1)
                ph = slice(64 * (hd % 2), 64 * (hd % 2) + 64)
                if u >= 2:
                    pe.wait_ge(sem("score_ready"), u - 1)
                b = bank[4 + u % 2]
                pe.matmul(b[:, 0:nk], qT[ph, hd // 2, qt * P:(qt + 1) * P], kT[ph, hd // 2, 0:nk], start=True,
                          stop=True)
                pe.matmul(b[:, nk - P:nk], identb[:, :], mask_ts[:, :], start=False, stop=True,
                          skip_group_check=True).then_inc(sem("qk_done"), 1)

            def key_tiles(qt):
                return [(2, META, 0)] + [(t, P, META + P * t) for t in range(qt + 1)]

            def probs_tr(u):
                hd, qt = divmod(u, 2)
                pe.wait_ge(sem("prob_ready"), u + 1)
                if u >= 2:
                    pe.wait_ge(sem(f"pt_read{qt}"), hd)
                for t, rows, c0 in key_tiles(qt):
                    ins = pe.transpose(bank[6 + u % 2][0:rows, t * P:(t + 1) * P], prb[u % 2][:, c0:c0 + rows],
                                       ident[:, :])
                ins.then_inc(sem("pt_done"), 1)

            def pv(u):
                hd, qt = divmod(u, 2)
                pe.wait_ge(sem(f"pt_read{qt}"), hd + 1)
                tl = key_tiles(qt)
                o = bank[2 * qt + hd // 8][:, (hd % 8) * FHD:(hd % 8 + 1) * FHD]
                for m, (t, rows, _) in enumerate(tl):
                    ins = pe.matmul(o, ptb[u % 2][0:rows, t, :], v1[0:rows, t, hd * FHD:(hd + 1) * FHD],
                                    start=(m == 0), stop=(m == len(tl) - 1))
                ins.then_inc(sem("pv_done"), 1)

            pe.wait_ge(sem("identb_ready"), 1)
            for u in range(NU + 3):
                if u < NU:
                    qk(u)
                if 1 <= u <= NU:
                    probs_tr(u - 1)
                if u >= 3:
                    pv(u - 3)
            pe.wait_ge(sem("o_ready"), 1)
            row_tr("ht1", TILES[:2], META)
            for b in (0, 1):
                pe.wait_ge(*read("tr", "ht1", b, 4))
            for j in range(9):
                if j < 8:
                    project("out1", j, xT, SEQ)
                if j >= 1:
                    col_tr("add1", "out1", j - 1, TILES[:2], META)
            moe(1)


_INS = ["x", "meta_tokens", "norm_mix", "norm_ffn", "m_w_in", "m_b_gate", "m_g_out", "m_w_out", "kv_norm", "kv_w",
        "kv_b_f", "k_norm", "f_w_q", "f_q_norm", "f_w_o", "moe_w_group", "moe_b_group", "moe_w_router",
        "moe_b_router", "moe_w_gate", "moe_w_up", "moe_w_down"]


def kernel(**inputs):
    import numpy as np
    import concourse.bacc as bacc
    from concourse.bass_utils import run_bass_kernel_spmd

    nc = bacc.Bacc("TRN2", target_bir_lowering=False, num_devices=1)
    arrays, io = {}, {}
    for name in _INS:
        a = np.ascontiguousarray(inputs[name])
        arrays["in_" + name] = a
        io[name] = nc.dram_tensor("in_" + name, a.shape, mybir.dt.from_np(a.dtype), kind="ExternalInput").ap()
    out = nc.dram_tensor("out_0", (1, SEQ, D), F32, kind="ExternalOutput").ap()
    build(nc, io, out)
    r = run_bass_kernel_spmd(nc, [arrays], core_ids=[0])
    return r.results[0]["out_0"]
```

```python
import concourse.bass as bass
from concourse import mybir
from contextlib import ExitStack

F32 = mybir.dt.float32
BF16 = mybir.dt.bfloat16
I32 = mybir.dt.int32
ALU = mybir.AluOpType
ACT = mybir.ActivationFunctionType
AX = mybir.AxisListType

P = 128
D = 1024
KB = D // P
SEQ = 256
META = 16
NT = SEQ + META
EPS = 1e-6
NEG = -1e30
TILES = [(0, 128, META), (1, 128, META + 128), (2, META, 0)]
MH, MDK, MDV = 4, 128, 256
GATE_CAP = 15.0
FH, FHD = 16, 64
NE, NG, EPG = 16, 4, 4
FE = 256
CAP = 64
OVF = (NT + CAP - 1) // CAP - 1
XROWS = 2 * NT + (OVF + 1) * CAP
HALF = D // 2
UC = 256
RING = 12
EU = 3
GRP = RING // EU


def build(nc, io, out):
    ctx = ExitStack()
    with ctx:
        def sb(name, shape, dt=F32):
            return ctx.enter_context(nc.sbuf_tensor(name, shape, dt))

        sems = {}

        def sem(name):
            if name not in sems:
                sems[name] = ctx.enter_context(nc.semaphore(name))
            return sems[name]

        ring = sb("ring", [P, RING, KB * UC])
        h = sb("h", [P, 3, D])
        xr = sb("xr", [P, 3, D])
        xT = sb("xT", [P, KB, NT])
        qk_area = sb("qk_area", [P, 2, KB * NT])
        qT = qk_area[:, 0, :].rearrange("p (j t) -> p j t", t=NT)
        kT = qk_area[:, 1, :].rearrange("p (j t) -> p j t", t=NT)
        xg = [qk_area[:, 0, b * HALF:(b + 1) * HALF] for b in range(GRP)]
        ye = [qk_area[:, 1, b * HALF:(b + 1) * HALF] for b in range(GRP)]
        gate_area = sb("gate_area", [P, FH * NT])
        sgoT = gate_area[:, 0:KB * NT].rearrange("p (j t) -> p j t", t=NT)
        cspB = gate_area[:, :].rearrange("p (h t) -> p h t", t=NT)
        xgT = [gate_area[:, i * 512:(i + 1) * 512].rearrange("p (q s) -> p q s", s=CAP) for i in (0, 1)]
        sg = [gate_area[:, 1024 + i * P:1024 + (i + 1) * P] for i in (0, 1)]
        arow = [gate_area[:, 1280 + i * P:1280 + (i + 1) * P] for i in (0, 1)]
        actT = [gate_area[:, 1536 + i * P:1536 + (i + 1) * P] for i in (0, 1)]
        WL = NT + SEQ + 128
        wexp = sb("wexp", [P, MH, WL])
        scb = [wexp[:, 0, i * NT:(i + 1) * NT] for i in (0, 1)]
        prb = [wexp[:, 1, i * NT:(i + 1) * NT] for i in (0, 1)]
        ptb = [wexp[:, 2 + i, 0:3 * 128].rearrange("p (t c) -> p t c", t=3) for i in (0, 1)]
        big = sb("big", [P, 6 * D + 3 * MH])
        hn = big[:, 0:3 * D].rearrange("p (t d) -> p t d", t=3)
        xqT = big[:, 0:KB * SEQ].rearrange("p (j t) -> p j t", t=SEQ)
        v0 = big[:, 3 * D:6 * D + 3 * MH].rearrange("p (t h e) -> p t h e", t=3, h=MH)
        v1 = big[:, 3 * D:6 * D].rearrange("p (t d) -> p t d", t=3)
        gat = big[:, 0:6 * D].rearrange("p (t c d) -> p t c d", t=3, c=2)
        ox = big[:, 0:HALF]
        oy = big[:, HALF:D]
        oxT = big[:, D:D + 512].rearrange("p (q s) -> p q s", s=CAP)
        osg, oarow, oactT = [big[:, D + 512 + i * P:D + 512 + (i + 1) * P] for i in range(3)]
        colT = [sb(f"colT{i}", [P, NT]) for i in (0, 1)]
        sq = [wexp[:, 2 + i, 384:384 + NT] for i in (0, 1)]

        ident = sb("ident", [P, P])
        identb = sb("identb", [P, P], BF16)
        mask_st = big[:, 512:512 + NT]
        negsel = big[0:MH, 0:512].rearrange("p (h c) -> p h c", h=MH)
        mask_ts = sb("mask_ts", [P, P], BF16)
        upper = sb("upper", [P, P], BF16)
        onesb = sb("onesb", [P, P], BF16)
        pair_ones = sb("pair_ones", [P, P])
        ones16 = sb("ones16", [P, NE])
        eps_col = sb("eps_col", [P, 1])
        scratch_i = sb("scratch_i", [P, EPG], I32)
        rev = sb("rev", [P, EPG])
        gains = sb("gains", [P, 5, KB])
        gains_x = sb("gains_x", [P, 2, KB])
        g_out = sb("g_out", [P, KB])
        gk = sb("gk", [P, 1])
        gq = sb("gq", [P, 1])
        w_gates = sb("w_gates", [P, KB, 2 * MH])
        b_gates = sb("b_gates", [P, 2 * MH])
        w_f = sb("w_f", [P, KB, FH])
        b_f = sb("b_f", [P, FH])
        w_rt = sb("w_rt", [P, 2, KB, NG + NE])
        b_rt = sb("b_rt", [P, 2, NG + NE])
        ss = sb("ss", [P, 3])
        rs = sb("rs", [P, 3])
        zg = sb("zg", [P, 3, FH])
        zg2 = sb("zg2", [P, 3, FH])
        zg3 = sb("zg3", [P, 3, FH])
        xr_flat = xr[:, :, :].rearrange("p t d -> p (t d)")
        row_li, row_sp, row_csp, row_c, row_M, row_m, onesrow = [
            xr_flat[0:n_, D + i * NT:D + (i + 1) * NT] for i, n_ in enumerate((MH, FH, FH, MH, MH, MH, FH))]
        tok_cm = sb("tok_cm", [P, 2, 3, MH])
        stile = xr[:, 0, 0:WL]
        den = sb("den", [P, 3, MH])
        den2 = sb("den2", [P, 3, MH])
        ssn = sb("ssn", [P, 3, MH])
        sums = sb("sums", [P, 2, FH])
        rsums = sb("rsums", [P, 2, FH])
        nmax = sb("nmax", [P, 2, FH])
        lg = sb("lg", [P, 3, NG + NE])
        gm = sb("gm", [P, 3, 1])
        t4 = sb("t4", [P, 3, 4])
        t4b = sb("t4b", [P, 3, 4])
        og = sb("og", [P, 3, NG])
        elg = sb("elg", [P, 3, EPG])
        o12 = sb("o12", [P, 2, 3, EPG])
        v12 = sb("v12", [P, 2, 3, 1])
        pg = sb("pg", [P, 3, 1])
        ex = sb("ex", [P, 3, 1])
        dn = sb("dn", [P, 3, 1])
        pe12 = sb("pe12", [P, 2, 3, 1])
        t16 = sb("t16", [P, 3, NE])
        e12 = sb("e12", [P, 2, 3, NE])
        eall = sb("eall", [P, 3, NE], BF16)
        cum = sb("cum", [P, NE])
        cnt = sb("cnt", [P, NE])
        slots = sb("slots", [P, 3, NE])
        idxf = sb("idxf", [P, 2, 3])
        idx = sb("idx", [P, 2, 3], I32)
        TBL_CNT, TBL_OVF = NE, 2 * NE
        tbl = sb("tbl", [1, TBL_OVF + NE], I32)
        novf = sb("novf", [1, NE])
        novf_sum = sb("novf_sum", [1, NE])

        bank = [ctx.enter_context(nc.psum_tensor(f"bank{i}", [P, 512], F32)) for i in range(8)]
        xs = [nc.dram_tensor(f"xs{l}", [XROWS, D], F32, kind="Internal").ap() for l in (0, 1)]
        ys = [nc.dram_tensor(f"ys{l}", [XROWS, D], F32, kind="Internal").ap() for l in (0, 1)]
        cs_dram = nc.dram_tensor("cs_dram", [FH, NT], F32, kind="Internal").ap()

        PH = {"q0": 4, "k0": 4, "v0": 8, "o0": 8, "out0": 8, "k1": 8, "v1": 8, "q1": 8, "out1": 8}
        PHASES = ["q0", "k0", "v0", "o0", "out0", "k1", "v1", "q1", "out1"]
        U_FIRST, u = {}, 0
        for ph in PHASES:
            if ph == "k1":
                u += NE * EU
            U_FIRST[ph] = u
            u += PH[ph] // 2
        U_MOE = [U_FIRST["out0"] + 4, U_FIRST["out1"] + 4]

        w_in, kv_w = io["m_w_in"][0], io["kv_w"]
        SRC = {"q0": (w_in, 0, "(p k) c -> p k c"), "k0": (w_in, 512, "(p k) c -> p k c"),
               "v0": (w_in, 1024, "(p k) c -> p k c"), "o0": (w_in, 2048, "(p k) c -> p k c"),
               "out0": (io["m_w_out"][0], 0, "(k p) c -> p k c"), "k1": (kv_w, 0, "(p k) c -> p k c"),
               "v1": (kv_w, D, "(p k) c -> p k c"), "q1": (io["f_w_q"][0], 0, "(p k) c -> p k c"),
               "out1": (io["f_w_o"][0], 0, "(k p) c -> p k c")}

        def unit(s):
            return ring[:, s % RING, :].rearrange("p (k c) -> p k c", c=UC)

        def unit_down(s):
            return ring[:, s % RING, :].rearrange("p (j d) -> p j d", d=D)

        def expert_units(s):
            return (s + 1, s + 2, s) if s % RING == RING - 1 else (s, s + 1, s + 2)

        def arrived(s):
            return sem(f"unit_arrived{s % RING}")

        TR = ["norm0", "vt0", "ht0", "add0", "ffn0", "norm1", "vt1", "ht1", "add1", "ffn1"]
        ORDER = {"proj": PHASES, "tr": TR}

        def before(kind, ph):
            return sum(PH.get(p, 8) for p in ORDER[kind][:ORDER[kind].index(ph)])

        def done(kind, ph, n):
            return sem(f"{kind}_done"), before(kind, ph) + n

        def read(kind, ph, b, n):
            return sem(f"{kind}_read{b}"), before(kind, ph) // 2 + n

        def wait_bank(pe, kind, ph, j):
            if before(kind, ph) + j >= 2:
                pe.wait_ge(*read(kind, ph, j % 2, j // 2))

        def alone(eng):
            eng.sem_inc(sem("wait_holder"), 1)

        block = ctx.enter_context(nc.Block())

        @block.sync
        def _(sp):
            def projection_is_through(old):
                for ph in PHASES:
                    if U_FIRST[ph] <= old < U_FIRST[ph] + PH[ph] // 2:
                        sp.wait_ge(*done("proj", ph, 2 * (old - U_FIRST[ph] + 1)))

            def load_units(ph):
                w, c0, lay = SRC[ph]
                for i in range(PH[ph] // 2):
                    s = U_FIRST[ph] + i
                    old = s - RING
                    projection_is_through(old)
                    if U_MOE[0] <= old < U_FIRST["k1"]:
                        e, part = divmod(old - U_MOE[0], EU)
                        sp.wait_ge(sem("down_done0"), e + 1 if part == 2 else max(e, 1))
                    sp.dma_start(unit(s), w[:, c0 + i * UC:c0 + (i + 1) * UC].rearrange(lay, k=KB)).then_inc(arrived(s), 16)

            def load_expert(l, e, s):
                for u, w in zip(expert_units(s)[:2], (io["moe_w_gate"], io["moe_w_up"])):
                    sp.dma_start(ring[:, u % RING, :].rearrange("p (h x) -> p h x", h=2),
                                 w[l, e, :, :].rearrange("(h p j) c -> p h (j c)", h=2, p=P)).then_inc(arrived(u), 16)

            def load_down(l, e, s):
                u = expert_units(s)[2]
                sp.dma_start(unit_down(u), io["moe_w_down"][l, e, :, :].rearrange("(j p) d -> p j d", p=P)) \
                    .then_inc(arrived(u), 16)

            def load_moe(l):
                base = U_MOE[l]
                for e in range(GRP):
                    for part, u in enumerate(expert_units(base + EU * e)):
                        projection_is_through(u - RING)
                        if part == 1:
                            load_expert(l, e, base + EU * e)
                        if part == 2:
                            load_down(l, e, base + EU * e)
                with sp.Fori(1, NE // GRP) as g:
                    for j in range(GRP):
                        if j == 0:
                            sp.wait_ge(sem(f"down_done{l}"), GRP * (g - 1) + 1)
                        else:
                            sp.wait_ge(sem(f"down_done{l}"), GRP * (g - 1) + j)
                        load_expert(l, GRP * g + j, base + EU * j)
                        sp.wait_ge(sem(f"down_done{l}"), GRP * (g - 1) + j + 1)
                        load_down(l, GRP * g + j, base + EU * j)

            for t in (0, 1):
                sp.dma_start(h[:, t, :], io["x"][0, t * P:(t + 1) * P, :]).then_inc(sem(f"x_loaded{t}"), 16)
            sp.dma_start(h[0:META, 2, :], io["meta_tokens"]).then_inc(sem("x_loaded2"), 16)
            with nc.allow_non_contiguous_dma(reason="small parameter vectors"):
                for i, g in enumerate((io["norm_mix"][0], io["norm_ffn"][0], io["kv_norm"], io["norm_mix"][1],
                                       io["norm_ffn"][1])):
                    sp.dma_start(gains[:, i, :], g.rearrange("(p k) -> p k", k=KB)).then_inc(sem("small_loaded"), 16)
                sp.dma_start(w_gates[:, :, :], w_in[:, 3072:3080].rearrange("(p k) c -> p k c", k=KB)) \
                    .then_inc(sem("small_loaded"), 16)
                sp.dma_start(b_gates[:, :], io["m_b_gate"][0].partition_broadcast(P)) \
                    .then_inc(sem("small_loaded"), 16)
            for ph in PHASES[:3]:
                load_units(ph)
            with nc.allow_non_contiguous_dma(reason="small parameter vectors"):
                sp.dma_start(g_out[:, :], io["m_g_out"][0].rearrange("h (j p) -> p (h j)", p=P)) \
                    .then_inc(sem("small2_loaded"), 16)
                for l in (0, 1):
                    for half in (0, 1):
                        sp.dma_start(gains_x[:, l, half:KB:2],
                                      io["norm_ffn"][l][HALF * half:HALF * (half + 1)].rearrange("(p j) -> p j", p=P)) \
                            .then_inc(sem("small2_loaded"), 16)
                for half in (0, 1):
                    sp.dma_start(gk[64 * half:64 * half + 64, :], io["k_norm"].rearrange("(p o) -> p o", o=1)) \
                        .then_inc(sem("small2_loaded"), 16)
                    sp.dma_start(gq[64 * half:64 * half + 64, :], io["f_q_norm"][0].rearrange("(p o) -> p o", o=1)) \
                        .then_inc(sem("small2_loaded"), 16)
                sp.dma_start(w_f[:, :, :], kv_w[:, 2 * D:2 * D + FH].rearrange("(p k) c -> p k c", k=KB)) \
                    .then_inc(sem("small2_loaded"), 16)
                sp.dma_start(b_f[:, :], io["kv_b_f"].partition_broadcast(P)).then_inc(sem("small2_loaded"), 16)
                for l in (0, 1):
                    sp.dma_start(w_rt[:, l, :, 0:NG], io["moe_w_group"][l].rearrange("(p k) c -> p k c", k=KB)) \
                        .then_inc(sem("small2_loaded"), 16)
                    sp.dma_start(w_rt[:, l, :, NG:NG + NE], io["moe_w_router"][l].rearrange("(p k) c -> p k c", k=KB)) \
                        .then_inc(sem("small2_loaded"), 16)
                    sp.dma_start(b_rt[:, l, 0:NG], io["moe_b_group"][l].partition_broadcast(P)) \
                        .then_inc(sem("small2_loaded"), 16)
                    sp.dma_start(b_rt[:, l, NG:NG + NE], io["moe_b_router"][l].partition_broadcast(P)) \
                        .then_inc(sem("small2_loaded"), 16)
            for ph in PHASES[3:5]:
                load_units(ph)
            load_moe(0)
            for t in range(3):
                sp.wait_ge(sem(f"gathered0_{t}"), 32)
            for ph in PHASES[5:]:
                load_units(ph)
            load_moe(1)
            for t in (0, 1):
                sp.wait_ge(sem("result_ready"), t + 1)
                sp.dma_start(out[0, t * P:(t + 1) * P, :], h[:, t, :]).then_inc(sem("out_written"), 16)
            sp.wait_ge(sem("out_written"), 32)

        @block.gpsimd
        def _(pool):
            pool.memset(ident[:, :], 0.0).then_inc(sem("pool_c"), 1)
            pool.memset(mask_st[:, :], 0.0).then_inc(sem("pool_c"), 1)
            pool.memset(mask_ts[:, :], 0.0).then_inc(sem("pool_c"), 1)
            pool.memset(upper[:, :], 1.0).then_inc(sem("pool_c"), 1)
            pool.memset(negsel[:, :, :], 0.0).then_inc(sem("pool_c"), 1)
            pool.memset(pair_ones[:, :], 1.0).then_inc(sem("pool_c"), 1)
            pool.wait_ge(sem("pool_c"), 6)
            pool.affine_select(out=ident[:, :], in_=ident[:, :], compare_op=ALU.not_equal, fill=1.0, base=0,
                               pattern=[[-1, P]], channel_multiplier=1).then_inc(sem("ident_ready"), 1)
            pool.affine_select(out=pair_ones[:, 0:64], in_=pair_ones[:, 0:64], compare_op=ALU.is_ge, fill=0.0,
                               base=63, pattern=[[0, 64]], channel_multiplier=-1).then_inc(sem("pool_c"), 1)
            pool.affine_select(out=pair_ones[:, 64:P], in_=pair_ones[:, 64:P], compare_op=ALU.is_ge, fill=0.0,
                               base=-64, pattern=[[0, 64]], channel_multiplier=1).then_inc(sem("pool_c"), 1)
            pool.affine_select(out=mask_st[:, :], in_=mask_st[:, :], compare_op=ALU.is_ge, fill=NEG, base=0,
                               pattern=[[1, NT]], channel_multiplier=-1).then_inc(sem("pool_c"), 1)
            pool.affine_select(out=mask_ts[:, :], in_=mask_ts[:, :], compare_op=ALU.is_ge, fill=NEG, base=0,
                               pattern=[[-1, P]], channel_multiplier=1).then_inc(sem("pool_c"), 1)
            pool.affine_select(out=upper[:, :], in_=upper[:, :], compare_op=ALU.is_gt, fill=0.0, base=0,
                               pattern=[[1, P]], channel_multiplier=-1).then_inc(sem("pool_c"), 1)
            pool.affine_select(out=negsel[:, :, :], in_=negsel[:, :, :], compare_op=ALU.not_equal, fill=-1.0,
                               base=0, pattern=[[-1, MH], [0, P]], channel_multiplier=1).then_inc(sem("pool_c"), 1)
            pool.memset(onesb[:, :], 1.0).then_inc(sem("pool_c"), 1)
            pool.wait_ge(sem("pool_c"), 13)
            pool.iota(scratch_i[:, :], pattern=[[-1, EPG]], base=EPG, channel_multiplier=0) \
                .then_inc(sem("pool_c"), 1)
            pool.wait_ge(sem("pool_c"), 14)
            pool.tensor_copy(rev[:, :], scratch_i[:, :]).then_inc(sem("consts_ready"), 1)
            for l, nt in ((0, NT), (1, SEQ)):
                for rows in (xs[l], ys[l]):
                    pool.dma_start(rows[2 * nt:2 * nt + CAP, :], io["x"][0, 0:CAP, :]).then_inc(sem("slack_written"), 16)

            def moe(l):
                tiles = TILES[:3 - l]
                nscat = 2 * len(tiles)
                pool.wait_ge(sem(f"idx_ready{l}"), 1)
                for t, rows, _ in tiles:
                    for c in (0, 1):
                        pool.indirect_dma_start(
                            out=xs[l], out_offset=bass.IndirectOffsetOnAxis(ap=idx[0:rows, c, t:t + 1], axis=0),
                            in_=xr[0:rows, t, :], in_offset=None).then_inc(sem(f"scattered{l}"), 16)
                pool.wait_ge(sem("slack_written"), 64)
                pool.wait_ge(sem(f"scattered{l}"), 16 * nscat)
                pool.wait_ge(sem(f"tbl_ready{l}"), 1)

                def load_x(b, e):
                    first = pool.value_load(tbl[0:1, bass.ds(e, 1)], min_val=0, max_val=2 * NT)
                    pool.dma_start(xg[b],
                                   xs[l][bass.ds(first, CAP), :].rearrange("s (h c) -> h s c", h=2)) \
                        .then_inc(sem(f"x_in{l}_{b}"), 16)

                def overflow(i):
                    n = pool.value_load(tbl[0:1, bass.ds(TBL_CNT + i, 1)], min_val=0, max_val=NT)
                    with pool.If(n > CAP):
                        before_i = pool.value_load(tbl[0:1, bass.ds(TBL_OVF + i, 1)], min_val=0, max_val=NE * OVF)
                        with pool.Fori(1, OVF + 1) as tt:
                            k = before_i + tt
                            with pool.If(n > CAP * tt):
                                first = pool.value_load(tbl[0:1, bass.ds(i, 1)], min_val=0, max_val=2 * NT)
                                for half in (0, 1):
                                    pool.dma_start(ox[CAP * half:CAP * (half + 1), :],
                                                   xs[l][bass.ds(first + CAP * tt, CAP), HALF * half:HALF * (half + 1)]) \
                                        .then_inc(sem(f"ox_in{l}"), 16)
                                pool.wait_ge(sem(f"ovf_dve{l}"), 4 * k)
                                alone(pool)
                                for half in (0, 1):
                                    pool.dma_start(ys[l][bass.ds(first + CAP * tt, CAP), HALF * half:HALF * (half + 1)],
                                                   oy[CAP * half:CAP * (half + 1), :]) \
                                        .then_inc(sem(f"oy_written{l}"), 16)
                                pool.wait_ge(sem(f"oy_written{l}"), 32 * k)
                                alone(pool)

                def write_y(b, e, first_one=False):
                    pool.wait_ge(sem(f"y_read{l}"), e + 1)
                    if not first_one:
                        pool.wait_ge(sem(f"y_written{l}"), 16 * e)
                    first = pool.value_load(tbl[0:1, bass.ds(e, 1)], min_val=0, max_val=2 * NT)
                    pool.dma_start(ys[l][bass.ds(first, CAP), :].rearrange("s (h c) -> h s c", h=2),
                                   ye[b]).then_inc(sem(f"y_written{l}"), 16)

                def turn(i, s, load=True, y=True, first_one=False):
                    if load:
                        pool.wait_ge(sem(f"tx_done{l}"), i + 1)
                        load_x(s, i + GRP)
                    overflow(i)
                    if y:
                        write_y((s - 1) % GRP, i - 1, first_one)

                for b in range(GRP):
                    load_x(b, b)
                for i in range(GRP):
                    turn(i, i, y=i >= 1, first_one=i == 1)
                with pool.Fori(1, NE // GRP - 1) as g:
                    for s in range(GRP):
                        turn(GRP * g + s, s)
                for i in range(NE - GRP, NE):
                    turn(i, i % GRP, load=False)
                write_y((NE - 1) % GRP, NE - 1)
                pool.wait_ge(sem(f"y_written{l}"), 16 * NE)
                for t, rows, _ in tiles:
                    for c in (0, 1):
                        pool.indirect_dma_start(
                            out=gat[0:rows, t, c, :], out_offset=None, in_=ys[l][0:2 * NT + CAP if l == 0 else 2 * SEQ + CAP, :],
                            in_offset=bass.IndirectOffsetOnAxis(ap=idx[0:rows, c, t:t + 1], axis=0)) \
                            .then_inc(sem(f"gathered{l}_{t}"), 16)

            moe(0)
            pool.wait_ge(sem("csp1_ready"), 1)
            pool.dma_start(cs_dram, row_csp[:, :]).then_inc(sem("cs_out"), 16)
            pool.wait_ge(sem("cs_out"), 16)
            pool.dma_start(cspB, cs_dram.partition_broadcast(P)).then_inc(sem("cspB_ready"), 16)
            moe(1)

        @block.scalar
        def _(act):
            chain = [0]

            def link(ins):
                chain[0] += 1
                ins.then_inc(sem("act_chain"), 1)
                act.wait_ge(sem("act_chain"), chain[0])

            def inverse_rms(name, tiles, tile_ready=None):
                for t, rows, _ in tiles:
                    if tile_ready:
                        act.wait_ge(*tile_ready(t))
                    ins = act.activation(gate_area[0:rows, t * D:(t + 1) * D], h[0:rows, t, :], ACT.Square,
                                         accum_out=ss[0:rows, t:t + 1])
                link(ins)
                link(act.activation(rs[:, :], ss[:, :], ACT.Ln, bias=eps_col[:, :], scale=1.0 / D))
                act.activation(rs[:, :], rs[:, :], ACT.Exp, scale=-0.5).then_inc(sem(f"rs_{name}"), 1)

            def norm_evac(ph, g, n=NT):
                for j in range(1, KB, 2):
                    act.wait_ge(*done("tr", ph, j + 1))
                    act.activation(xT[:, j, 0:n], bank[3][:, 0:n], ACT.Copy, scale=gains[:, g, j:j + 1]) \
                        .then_inc(sem("tr_read1"), 1)

            def load_exp_ln():
                act.preload_act_table_set("natural_log_exp_and_others")

            load_exp_ln()
            act.wait_ge(sem("init_ready"), 1)
            inverse_rms("norm0", TILES, lambda t: (sem(f"x_loaded{t}"), 16))
            act.wait_ge(sem("small_loaded"), 16 * 7)
            norm_evac("norm0", 0)
            act.wait_ge(sem("gate_z"), 1)
            act.activation(zg2[:, :, 0:8], zg[:, :, 0:8], ACT.Exp, scale=2.0 / GATE_CAP).then_inc(sem("gate_e"), 1)
            act.wait_ge(sem("gate_g"), 1)
            link(act.activation(zg2[:, :, 4:8], zg[:, :, 4:8], ACT.Exp, scale=-1.0))
            act.activation(zg[:, :, 4:8], zg2[:, :, 4:8], ACT.Ln, bias=1.0).then_inc(sem("gate_sp"), 1)
            for j in range(PH["q0"]):
                act.wait_ge(*done("proj", "q0", j + 1))
                act.activation(qT[:, j, :], bank[j % 2][:, 0:NT], ACT.Copy, scale=MDK ** -0.5) \
                    .then_inc(sem(f"proj_read{j % 2}"), 1)
            act.wait_ge(sem("cm_tok"), 1)
            act.activation(tok_cm[:, 1, :, :], tok_cm[:, 1, :, :], ACT.Exp, scale=-1.0).then_inc(sem("expm_ready"), 1)
            for hd in range(MH):
                act.wait_ge(sem("warg"), hd + 1)
                link(act.activation(wexp[0:META, hd, 0:NT], wexp[0:META, hd, 0:NT], ACT.Exp))
                act.activation(wexp[:, hd, NT:WL], wexp[:, hd, NT:WL], ACT.Exp).then_inc(sem("wexp_ready"), 1)

            def pt_evac(u):
                act.wait_ge(sem("pt_done"), u + 1)
                if u >= 2:
                    act.wait_ge(sem("pv_done"), u - 1)
                src = bank[7][:, 0:384].rearrange("p (t c) -> p t c", t=3)
                act.activation(ptb[1][:, 0:2, :], src[:, 0:2, :], ACT.Copy)
                act.activation(ptb[1][0:META, 2, :], src[0:META, 2, :], ACT.Copy).then_inc(sem("pt_read1"), 1)

            def v_evac(l, dst2):
                for j in range(8):
                    act.wait_ge(*done("tr", f"vt{l}", j + 1))
                    src = bank[2 + j % 2][:, 0:384].rearrange("p (t c) -> p t c", t=3)
                    act.activation(dst2(j, slice(0, P), slice(0, 2)), src[:, 0:2, :], ACT.Copy)
                    act.activation(dst2(j, slice(0, META), 2), src[0:META, 2, :], ACT.Copy) \
                        .then_inc(sem(f"tr_read{j % 2}"), 1)

            v_evac(0, lambda j, p, t: v0[p, t, j // 2, (j % 2) * P:(j % 2) * P + P])
            for j in range(8):
                act.wait_ge(*done("proj", "o0", j + 1))
                act.activation(sgoT[:, j, :], bank[j % 2][:, 0:NT], ACT.Sigmoid) \
                    .then_inc(sem(f"proj_read{j % 2}"), 1)
            load_exp_ln()
            for hd in range(MH):
                act.wait_ge(sem("num_done"), hd + 1)
                for t, rows, _ in TILES:
                    ins = act.activation(hn[0:rows, t, hd * MDV:(hd + 1) * MDV], bank[(0, 1, 2)[t]][0:rows, 0:MDV],
                                         ACT.Copy)
                ins.then_inc(sem("num_read_act"), 1)
                act.wait_ge(sem("num_read_act"), hd + 1)
                for t, rows, _ in TILES:
                    dump = (colT[0][:, 0:MDV], colT[1][:, 0:MDV], xr_flat[0:META, 2 * D:2 * D + MDV])[t]
                    ins = act.activation(dump, hn[0:rows, t, hd * MDV:(hd + 1) * MDV], ACT.Square,
                                         accum_out=ssn[0:rows, t, hd:hd + 1])
                ins.then_inc(sem("ssn_ready"), 1)
            act.wait_ge(sem("den2_ready"), 1)
            link(act.activation(ssn[:, :, :], den2[:, :, :], ACT.Ln))
            act.activation(ssn[:, :, :], ssn[:, :, :], ACT.Exp, scale=-0.5).then_inc(sem("hscale"), 1)

            def out_evac(l, n):
                for j in range(8):
                    act.wait_ge(*done("proj", f"out{l}", j + 1))
                    if j >= 2:
                        act.wait_ge(*done("tr", f"add{l}", j - 1))
                    act.activation(colT[j % 2][:, 0:n], bank[j % 2][:, 0:n], ACT.Copy) \
                        .then_inc(sem(f"proj_read{j % 2}"), 1)

            out_evac(0, NT)

            def moe(l):
                tiles = TILES[:3 - l]
                for b in (0, 1):
                    act.wait_ge(*read("tr", f"add{l}", b, 4))
                inverse_rms(f"ffn{l}", tiles)
                norm_evac(f"ffn{l}", 1 if l == 0 else 4, NT if l == 0 else SEQ)
                act.wait_ge(sem(f"gl_sub{l}"), 1)
                act.activation(t4b[:, :, :], t4[:, :, :], ACT.Exp).then_inc(sem(f"gl_exp{l}"), 1)
                act.wait_ge(sem(f"v_sub{l}"), 1)
                act.activation(ex[:, :, :], dn[:, :, :], ACT.Exp).then_inc(sem(f"v_exp{l}"), 1)
                act.preload_act_table(ACT.Silu)
                act.wait_ge(sem(f"tbl_ready{l}"), 1)

                def overflow(i):
                    n = act.value_load(tbl[0:1, bass.ds(TBL_CNT + i, 1)], min_val=0, max_val=NT)
                    with act.If(n > CAP):
                        before_i = act.value_load(tbl[0:1, bass.ds(TBL_OVF + i, 1)], min_val=0, max_val=NE * OVF)
                        with act.Fori(1, OVF + 1) as tt:
                            k = before_i + tt
                            with act.If(n > CAP * tt):
                                act.wait_ge(sem(f"ovf_pe{l}"), 4 * k - 2)
                                act.activation(osg, bank[7][:, 0:128], ACT.Silu).then_inc(sem(f"ovf_act{l}"), 1)
                                act.wait_ge(sem(f"ovf_act{l}"), k)
                                alone(act)

                def turn(i, s, experts=True, y=True, wait_buf=True):
                    if experts:
                        act.wait_ge(sem(f"gu_done{l}"), i + 1)
                        act.activation(sg[s % 2], bank[1 + s % 2][:, 0:P], ACT.Silu).then_inc(sem(f"silu_done{l}"), 1)
                        overflow(i)
                    if y:
                        if wait_buf:
                            act.wait_ge(sem(f"y_written{l}"), 16 * (i - 3))
                        act.wait_ge(sem(f"down_done{l}"), i)
                        act.activation(ye[(s - 1) % GRP], bank[3 + (s + 1) % 2][:, :], ACT.Copy) \
                            .then_inc(sem(f"y_read{l}"), 1)

                for i in range(GRP):
                    turn(i, i, y=i >= 1, wait_buf=False)
                with act.Fori(1, NE // GRP) as g:
                    for s in range(GRP):
                        turn(GRP * g + s, s)
                turn(NE, 0, experts=False)

            moe(0)
            load_exp_ln()
            inverse_rms("norm1", TILES, lambda t: (sem("combined0"), t + 1))
            for j in range(1, KB, 2):
                act.wait_ge(*done("tr", "norm1", j + 1))
                act.activation(xT[:, j, :], bank[3][:, 0:NT], ACT.Copy, scale=gains[:, 2, j:j + 1])
                act.activation(xqT[:, j, :], bank[3][:, META:NT], ACT.Copy, scale=gains[:, 3, j:j + 1]) \
                    .then_inc(sem("tr_read1"), 1)
            act.wait_ge(sem("f_abs"), 1)
            link(act.activation(zg2[:, :, :], zg2[:, :, :], ACT.Exp, scale=-1.0))
            act.activation(zg2[:, :, :], zg2[:, :, :], ACT.Ln, bias=1.0).then_inc(sem("f_ln"), 1)

            def head_norm(ph, n):
                for j in range(8):
                    act.wait_ge(*done("proj", ph, j + 1))
                    if j >= 2:
                        act.wait_ge(sem(f"hn_done_{ph}"), j - 1)
                    act.activation(colT[j % 2][:, 0:n], bank[j % 2][:, 0:n], ACT.Copy)
                    act.activation(sq[j % 2][:, 0:n], bank[j % 2][:, 0:n], ACT.Square) \
                        .then_inc(sem(f"proj_read{j % 2}"), 1)
                    act.wait_ge(sem(f"ssq_done_{ph}"), j + 1)
                    link(act.activation(sq[j % 2][:, 0:n], bank[4 + j % 2][:, 0:n], ACT.Ln, bias=eps_col[:, :],
                                        scale=1.0 / FHD))
                    act.activation(sq[j % 2][:, 0:n], sq[j % 2][:, 0:n], ACT.Exp, scale=-0.5) \
                        .then_inc(sem(f"rstd_{ph}"), 1)

            head_norm("k1", NT)
            v_evac(1, lambda j, p, t: v1[p, t, j * P:(j + 1) * P])
            head_norm("q1", SEQ)
            for u in range(2 * FH):
                hd, qt = divmod(u, 2)
                nk = META + P * (qt + 1)
                act.wait_ge(sem("score_ready"), u + 1)
                if u >= 2:
                    act.wait_ge(sem("pt_done"), u - 1)
                act.activation(prb[u % 2][:, 0:nk], scb[u % 2][:, 0:nk], ACT.Exp, scale=-1.0,
                               bias=nmax[:, qt, hd:hd + 1], accum_out=sums[:, qt, hd:hd + 1]) \
                    .then_inc(sem("prob_ready"), 1)
                if qt == 1 and u >= 3:
                    pt_evac(u - 2)
            pt_evac(2 * FH - 1)
            out_evac(1, SEQ)
            moe(1)

        @block.vector
        def _(dve):
            chain = [0]

            def link(ins):
                chain[0] += 1
                ins.then_inc(sem("dve_chain"), 1)
                dve.wait_ge(sem("dve_chain"), chain[0])

            dve.memset(v0[:, :, :, MDV:MDV + 1], 1.0)
            dve.memset(ss[:, :], 1.0)
            dve.memset(rs[:, :], 1.0)
            dve.memset(zg[:, :, :], 0.0)
            dve.memset(zg2[:, :, :], 0.0)
            dve.memset(lg[:, :, :], 0.0)
            dve.memset(slots[:, :, :], 0.0)
            dve.memset(ssn[:, :, :], 1.0)
            dve.memset(den[:, :, :], 1.0)
            dve.memset(tok_cm[:, :, :, :], 0.0)
            dve.memset(tbl[:, :], 0)
            dve.memset(ones16[:, :], 1.0)
            dve.memset(eps_col[:, :], EPS).then_inc(sem("init_ready"), 1)
            dve.wait_ge(sem("init_ready"), 1)

            def scale_rows(name, tiles):
                dve.wait_ge(sem(f"rs_{name}"), 1)
                for t, rows, _ in tiles:
                    dve.tensor_scalar(xr[0:rows, t, :], h[0:rows, t, :], rs[0:rows, t:t + 1], None, ALU.mult) \
                        .then_inc(sem(f"xr_{name}"), 1)

            def norm_evac(ph, g, n=NT):
                for j in range(0, KB, 2):
                    dve.wait_ge(*done("tr", ph, j + 1))
                    dve.tensor_scalar(xT[:, j, 0:n], bank[2][:, 0:n], gains[:, g, j:j + 1], None, ALU.mult) \
                        .then_inc(sem("tr_read0"), 1)

            scale_rows("norm0", TILES)
            dve.wait_ge(sem("small_loaded"), 16 * 7)
            norm_evac("norm0", 0)
            dve.wait_ge(sem("gate_mm"), 1)
            for t, rows, _ in TILES:
                ins = dve.tensor_tensor(zg[0:rows, t, 0:8], bank[4][0:rows, t * 8:t * 8 + 8], b_gates[0:rows, :],
                                        ALU.add)
            ins.then_inc(sem("gate_z"), 1)
            dve.wait_ge(sem("gate_e"), 1)
            link(dve.tensor_scalar(zg2[:, :, 0:8], zg2[:, :, 0:8], 1.0, None, ALU.add))
            link(dve.reciprocal(zg2[:, :, 0:8], zg2[:, :, 0:8]))
            dve.tensor_scalar(zg[:, :, 0:8], zg2[:, :, 0:8], -2 * GATE_CAP, GATE_CAP, ALU.mult, ALU.add) \
                .then_inc(sem("gate_g"), 1)
            dve.wait_ge(sem("gate_rows"), 1)
            dve.memset(onesrow[:, :], 1.0)
            dve.tensor_copy(row_li[:, :], bank[5][0:MH, 0:NT])
            link(dve.tensor_copy(row_sp[0:MH, :], bank[6][0:MH, 0:NT]))
            dve.wait_ge(sem("consts_ready"), 1)
            dve.tensor_copy(identb[:, :], ident[:, :]).then_inc(sem("identb_ready"), 1)
            link(dve.tensor_tensor_scan(row_csp[0:MH, :], onesrow[0:MH, :], row_sp[0:MH, :], 0.0, ALU.mult, ALU.add))
            link(dve.tensor_tensor(row_c[:, :], row_li[:, :], row_csp[0:MH, :], ALU.add))
            link(dve.tensor_tensor_scan(row_M[:, :], row_c[:, :], row_c[:, :], -3.0e38, ALU.max, ALU.max))
            dve.tensor_tensor(row_m[:, :], row_M[:, :], row_csp[0:MH, :], ALU.subtract).then_inc(sem("rows_ready"), 1)
            for j in range(PH["k0"]):
                dve.wait_ge(*done("proj", "k0", j + 1))
                dve.tensor_copy(kT[:, j, :], bank[j % 2][:, 0:NT]).then_inc(sem(f"proj_read{j % 2}"), 1)
            dve.wait_ge(sem("cm_mm"), 1)
            for t, rows, _ in TILES:
                ins = dve.tensor_copy(tok_cm[0:rows, :, t, :],
                                      bank[4][0:rows, t * 8:t * 8 + 8].rearrange("p (a b) -> p a b", a=2))
            ins.then_inc(sem("cm_tok"), 1)
            dve.wait_ge(sem("cm_tok"), 1)
            for hd in range(MH):
                dve.wait_ge(sem("negM_mm"), hd + 1)
                nm = bank[5 + hd % 2]
                dve.scalar_tensor_tensor(wexp[0:META, hd, 0:NT], nm[0:META, 0:NT], tok_cm[0:META, 0, 2, hd:hd + 1],
                                         mask_st[0:META, :], ALU.add, ALU.add)
                dve.scalar_tensor_tensor(wexp[:, hd, NT:NT + SEQ], nm[:, META:NT], tok_cm[:, 0, 0, hd:hd + 1],
                                         mask_st[:, 0:SEQ], ALU.add, ALU.add)
                dve.scalar_tensor_tensor(wexp[:, hd, NT + SEQ:WL], nm[:, META + P:NT], tok_cm[:, 0, 1, hd:hd + 1],
                                         mask_st[:, 0:P], ALU.add, ALU.add).then_inc(sem("warg"), 1)

            def col_evac(l, n):
                for j in range(8):
                    dve.wait_ge(*done("proj", f"v{l}", j + 1))
                    if j >= 2:
                        dve.wait_ge(*done("tr", f"vt{l}", j - 1))
                    dve.tensor_copy(colT[j % 2][:, 0:n], bank[j % 2][:, 0:n]).then_inc(sem(f"proj_read{j % 2}"), 1)

            def pt_evac(u):
                dve.wait_ge(sem("pt_done"), u + 1)
                if u >= 2:
                    dve.wait_ge(sem("pv_done"), u - 1)
                src = bank[6][:, 0:384].rearrange("p (t c) -> p t c", t=3)
                dve.tensor_copy(ptb[0][:, 0, :], src[:, 0, :])
                dve.tensor_copy(ptb[0][0:META, 2, :], src[0:META, 2, :]).then_inc(sem("pt_read0"), 1)

            col_evac(0, NT)
            for hd in range(MH):
                dve.wait_ge(sem("wexp_ready"), hd + 1)
                dve.wait_ge(sem("s_done"), hd + 1)
                if hd:
                    dve.wait_ge(sem("num_done"), hd)
                dve.tensor_tensor(stile[0:META, 0:NT], bank[4][0:META, 0:NT], wexp[0:META, hd, 0:NT], ALU.mult)
                dve.tensor_tensor(stile[:, NT:WL], bank[5][:, 0:WL - NT], wexp[:, hd, NT:WL], ALU.mult) \
                    .then_inc(sem("st_ready"), 1)
                dve.wait_ge(sem("num_done"), hd + 1)
                dve.wait_ge(sem("num_read_act"), hd + 1)
                for t, rows, _ in TILES:
                    ins = dve.tensor_copy(den[0:rows, t, hd:hd + 1], bank[t][0:rows, MDV:MDV + 1])
                ins.then_inc(sem("num_read"), 1)
            dve.wait_ge(sem("num_read"), MH)
            dve.wait_ge(sem("expm_ready"), 1)
            dve.wait_ge(sem("ssn_ready"), MH)
            link(dve.scalar_tensor_tensor(den2[:, :, :], den[:, :, :], -1.0, den[:, :, :], ALU.mult, ALU.max))
            link(dve.tensor_tensor(den2[:, :, :], den2[:, :, :], tok_cm[:, 1, :, :], ALU.max))
            link(dve.tensor_tensor(den2[:, :, :], den2[:, :, :], den2[:, :, :], ALU.mult))
            link(dve.tensor_scalar(den2[:, :, :], den2[:, :, :], EPS, None, ALU.mult))
            dve.scalar_tensor_tensor(den2[:, :, :], ssn[:, :, :], 1.0 / MDV, den2[:, :, :], ALU.mult, ALU.add) \
                .then_inc(sem("den2_ready"), 1)
            dve.wait_ge(sem("hscale"), 1)
            for t, rows, _ in TILES:
                for hd in range(MH):
                    c = slice(hd * MDV, (hd + 1) * MDV)
                    ins = dve.tensor_scalar(hn[0:rows, t, c], hn[0:rows, t, c], ssn[0:rows, t, hd:hd + 1], None,
                                            ALU.mult)
                ins.then_inc(sem("hn_ready"), 1)
            dve.wait_ge(sem("small2_loaded"), 16 * 19)
            for j in range(8):
                dve.wait_ge(*done("tr", "ht0", j + 1))
                dve.scalar_tensor_tensor(xT[:, j, :], bank[2 + j % 2][:, 0:NT], g_out[:, j:j + 1], sgoT[:, j, :],
                                         ALU.mult, ALU.mult).then_inc(sem(f"tr_read{j % 2}"), 1)

            def add_evac(l):
                for j in range(8):
                    dve.wait_ge(*done("tr", f"add{l}", j + 1))
                    src = bank[2 + j % 2][:, 0:384].rearrange("p (t c) -> p t c", t=3)
                    c = slice(j * P, (j + 1) * P)
                    if l == 0:
                        dve.tensor_tensor(h[0:META, 2, c], h[0:META, 2, c], src[0:META, 2, :], ALU.add)
                    ins = dve.tensor_tensor(h[:, 0:2, c], h[:, 0:2, c], src[:, 0:2, :], ALU.add)
                    ins.then_inc(sem(f"tr_read{j % 2}"), 1)
                dve.wait_ge(*read("tr", f"add{l}", 0, 4))
                dve.wait_ge(*read("tr", f"add{l}", 1, 4))

            add_evac(0)

            def route(l):
                tiles = TILES[:3 - l]
                scale_rows(f"ffn{l}", tiles)
                norm_evac(f"ffn{l}", 1 if l == 0 else 4, NT if l == 0 else SEQ)
                dve.wait_ge(sem(f"router_mm{l}"), 1)
                for t, rows, _ in tiles:
                    ins = dve.tensor_tensor(lg[0:rows, t, :], bank[4][0:rows, t * 20:t * 20 + 20], b_rt[0:rows, l, :],
                                            ALU.add)
                link(ins)
                bc3 = [P, 3, 4]
                revb = rev[:, :].unsqueeze(1).to_broadcast(bc3)

                def first_max(dst, src, mx):
                    link(dve.tensor_tensor(t4[:, :, :], src, mx.to_broadcast(bc3), ALU.is_equal))
                    link(dve.tensor_tensor(t4[:, :, :], t4[:, :, :], revb, ALU.mult))
                    link(dve.tensor_reduce(dn[:, :, :], t4[:, :, :], AX.X, ALU.max))
                    link(dve.tensor_tensor(dst, t4[:, :, :], dn[:, :, :].to_broadcast(bc3), ALU.is_equal))

                gl = lg[:, :, 0:NG]
                link(dve.tensor_reduce(gm[:, :, :], gl, AX.X, ALU.max))
                first_max(og[:, :, :], gl, gm[:, :, :])
                dve.tensor_tensor(t4[:, :, :], gl, gm[:, :, :].to_broadcast(bc3), ALU.subtract) \
                    .then_inc(sem(f"gl_sub{l}"), 1)
                dve.wait_ge(sem(f"gl_exp{l}"), 1)
                link(dve.tensor_reduce(pg[:, :, :], t4b[:, :, :], AX.X, ALU.add))
                link(dve.reciprocal(pg[:, :, :], pg[:, :, :]))
                el = lg[:, :, NG:NG + NE].rearrange("p t (g j) -> p t g j", g=NG)
                t16v = t16[:, :, :].rearrange("p t (g j) -> p t g j", g=NG)
                full = [P, 3, NG, EPG]
                ogb = og[:, :, :].unsqueeze(3).to_broadcast(full)
                link(dve.tensor_tensor(t16v, el, ogb, ALU.mult))
                link(dve.tensor_reduce(elg[:, :, :], t16v.rearrange("p t g j -> p t j g"), AX.X, ALU.add))
                link(dve.tensor_reduce(v12[:, 0, :, :], elg[:, :, :], AX.X, ALU.max))
                first_max(o12[:, 0, :, :], elg[:, :, :], v12[:, 0, :, :])
                link(dve.scalar_tensor_tensor(elg[:, :, :], o12[:, 0, :, :], NEG, elg[:, :, :], ALU.mult, ALU.add))
                link(dve.tensor_reduce(v12[:, 1, :, :], elg[:, :, :], AX.X, ALU.max))
                first_max(o12[:, 1, :, :], elg[:, :, :], v12[:, 1, :, :])
                dve.tensor_tensor(dn[:, :, :], v12[:, 1, :, :], v12[:, 0, :, :], ALU.subtract) \
                    .then_inc(sem(f"v_sub{l}"), 1)
                for c in (0, 1):
                    link(dve.tensor_tensor(e12[:, c, :, :].rearrange("p t (g j) -> p t g j", g=NG), ogb,
                                           o12[:, c, :, :].unsqueeze(2).to_broadcast(full), ALU.mult))
                dve.tensor_tensor(eall[:, :, :], e12[:, 0, :, :], e12[:, 1, :, :], ALU.add) \
                    .then_inc(sem(f"eall_ready{l}"), 1)
                dve.wait_ge(sem(f"v_exp{l}"), 1)
                link(dve.tensor_scalar(dn[:, :, :], ex[:, :, :], 1.0, None, ALU.add))
                link(dve.reciprocal(dn[:, :, :], dn[:, :, :]))
                link(dve.tensor_tensor(pe12[:, 0, :, :], dn[:, :, :], pg[:, :, :], ALU.mult))
                link(dve.tensor_tensor(pe12[:, 1, :, :], pe12[:, 0, :, :], ex[:, :, :], ALU.mult))
                dve.wait_ge(sem(f"pos_mm{l}"), 1)
                link(dve.tensor_copy(cnt[:, :], bank[4][:, 48:64]))
                link(dve.tensor_tensor_scan(cum[:, :], ones16[:, :], cnt[:, :], 0.0, ALU.mult, ALU.add))
                link(dve.tensor_tensor(cum[:, :], cum[:, :], cnt[:, :], ALU.subtract))
                for t, rows, _ in tiles:
                    ins = dve.tensor_tensor(slots[0:rows, t, :], bank[4][0:rows, t * 16:t * 16 + 16], cum[0:rows, :],
                                            ALU.add)
                link(ins)
                for c in (0, 1):
                    link(dve.tensor_tensor(t16[:, :, :], slots[:, :, :], e12[:, c, :, :], ALU.mult))
                    link(dve.tensor_reduce(idxf[:, c, :], t16[:, :, :], AX.X, ALU.add))
                dve.tensor_copy(idx[:, :, :], idxf[:, :, :]).then_inc(sem(f"idx_ready{l}"), 1)
                dve.tensor_copy(tbl[0:1, 0:NE], cum[0:1, :])
                dve.tensor_copy(tbl[0:1, TBL_CNT:TBL_CNT + NE], cnt[0:1, :])
                link(dve.tensor_scalar(novf[:, :], cnt[0:1, :], float(CAP), None, ALU.is_gt))
                for tt in range(2, OVF + 1):
                    link(dve.scalar_tensor_tensor(novf[:, :], cnt[0:1, :], float(CAP * tt), novf[:, :], ALU.is_gt,
                                                  ALU.add))
                link(dve.tensor_tensor_scan(novf_sum[:, :], ones16[0:1, :], novf[:, :], 0.0, ALU.mult, ALU.add))
                dve.tensor_tensor(tbl[0:1, TBL_OVF:TBL_OVF + NE], novf_sum[:, :], novf[:, :], ALU.subtract) \
                    .then_inc(sem(f"tbl_ready{l}"), 1)
                dve.wait_ge(sem(f"tbl_ready{l}"), 1)

            def moe(l):
                route(l)
                tiles = TILES[:3 - l]
                gb = gains_x[:, l, :].unsqueeze(2).to_broadcast([P, KB, CAP])

                def blocks(b):
                    return bank[b][:, :].rearrange("p (q s) -> p q s", s=CAP)

                def overflow(i):
                    n = dve.value_load(tbl[0:1, bass.ds(TBL_CNT + i, 1)], min_val=0, max_val=NT)
                    with dve.If(n > CAP):
                        before_i = dve.value_load(tbl[0:1, bass.ds(TBL_OVF + i, 1)], min_val=0, max_val=NE * OVF)
                        with dve.Fori(1, OVF + 1) as tt:
                            k = before_i + tt
                            with dve.If(n > CAP * tt):
                                od, op = sem(f"ovf_dve{l}"), sem(f"ovf_pe{l}")
                                dve.wait_ge(op, 4 * k - 3)
                                dve.tensor_tensor(oxT, blocks(7), gb, ALU.mult).then_inc(od, 1)
                                dve.wait_ge(sem(f"ovf_act{l}"), k)
                                dve.tensor_tensor(oarow, osg, bank[7][:, P:2 * P], ALU.mult).then_inc(od, 1)
                                dve.wait_ge(op, 4 * k - 1)
                                dve.tensor_copy(oactT, bank[7][:, 0:P]).then_inc(od, 1)
                                dve.wait_ge(op, 4 * k)
                                dve.tensor_copy(oy, bank[7][:, :]).then_inc(od, 1)
                                dve.wait_ge(od, 4 * k)
                                alone(dve)

                def x_evac(s, v):
                    dve.wait_ge(sem(f"tx_done{l}"), v)
                    dve.tensor_tensor(xgT[s % 2], blocks(0), gb, ALU.mult).then_inc(sem(f"xT_read{l}"), 1)

                def actT_evac(i, s):
                    dve.wait_ge(sem(f"at_done{l}"), i)
                    dve.tensor_copy(actT[(s + 1) % 2], bank[5 + (s + 1) % 2][:, 0:P]).then_inc(sem(f"at_read{l}"), 1)

                def turn(i, s, first=False, last=False):
                    if not first or s >= 1:
                        if not first or s >= 3:
                            dve.wait_ge(sem(f"down_done{l}"), i - 2)
                        actT_evac(i, s)
                    if not last:
                        x_evac(s + 1, i + 2)
                    if not first or s >= 2:
                        dve.wait_ge(sem(f"at_done{l}"), i - 1)
                    dve.wait_ge(sem(f"silu_done{l}"), i + 1)
                    dve.tensor_tensor(arow[s % 2], sg[s % 2], bank[1 + s % 2][:, P:2 * P], ALU.mult) \
                        .then_inc(sem(f"act_ready{l}"), 1)
                    overflow(i)

                x_evac(0, 1)
                for i in range(GRP):
                    turn(i, i, first=True)
                with dve.Fori(1, NE // GRP - 1) as g:
                    for s in range(GRP):
                        turn(GRP * g + s, s)
                for i in range(NE - GRP, NE):
                    turn(i, i % GRP, last=i == NE - 1)
                dve.wait_ge(sem(f"down_done{l}"), NE - 2)
                actT_evac(NE, 0)
                for t, rows, _ in tiles:
                    dve.wait_ge(sem(f"gathered{l}_{t}"), 32)
                    for c in (0, 1):
                        ins = dve.scalar_tensor_tensor(h[0:rows, t, :], gat[0:rows, t, c, :], pe12[0:rows, c, t, :],
                                                       h[0:rows, t, :], ALU.mult, ALU.add)
                        if c == 0:
                            link(ins)
                    ins.then_inc(sem("combined0" if l == 0 else "result_ready"), 1)

            moe(0)
            dve.wait_ge(sem("combined0"), 3)
            scale_rows("norm1", TILES)
            for j in range(0, KB, 2):
                dve.wait_ge(*done("tr", "norm1", j + 1))
                dve.tensor_scalar(xT[:, j, :], bank[2][:, 0:NT], gains[:, 2, j:j + 1], None, ALU.mult)
                dve.tensor_scalar(xqT[:, j, :], bank[2][:, META:NT], gains[:, 3, j:j + 1], None, ALU.mult) \
                    .then_inc(sem("tr_read0"), 1)
            dve.wait_ge(sem("f_mm"), 1)
            for t, rows, _ in TILES:
                ins = dve.tensor_tensor(zg[0:rows, t, :], bank[4][0:rows, t * FH:(t + 1) * FH], b_f[0:rows, :], ALU.add)
            link(ins)
            dve.scalar_tensor_tensor(zg2[:, :, :], zg[:, :, :], -1.0, zg[:, :, :], ALU.mult, ALU.max) \
                .then_inc(sem("f_abs"), 1)
            link(dve.tensor_scalar(zg3[:, :, :], zg[:, :, :], 0.0, None, ALU.min))
            dve.wait_ge(sem("f_ln"), 1)
            dve.tensor_tensor(zg[:, :, :], zg2[:, :, :], zg3[:, :, :], ALU.subtract).then_inc(sem("f_sp"), 1)
            dve.wait_ge(sem("f_rows"), 1)
            dve.memset(onesrow[:, :], 1.0)
            link(dve.tensor_copy(row_sp[:, :], bank[6][0:FH, 0:NT]))
            dve.tensor_tensor_scan(row_csp[:, :], onesrow[:, :], row_sp[:, :], 0.0, ALU.mult, ALU.add) \
                .then_inc(sem("csp1_ready"), 1)
            dve.tensor_scalar(gq[:, :], gq[:, :], FHD ** -0.5, None, ALU.mult).then_inc(sem("gq_scaled"), 1)
            dve.wait_ge(sem("gq_scaled"), 1)

            def head_norm(ph, dst, g, n):
                for j in range(8):
                    dve.wait_ge(sem(f"rstd_{ph}"), j + 1)
                    dve.scalar_tensor_tensor(dst[:, j, 0:n], colT[j % 2][:, 0:n], g[:, :], sq[j % 2][:, 0:n], ALU.mult,
                                             ALU.mult).then_inc(sem(f"hn_done_{ph}"), 1)

            head_norm("k1", kT, gk, NT)
            dve.wait_ge(sem("hn_done_k1"), 8)
            col_evac(1, NT)
            head_norm("q1", qT, gq, SEQ)
            dve.wait_ge(sem("cspB_ready"), 16)
            for u in range(2 * FH):
                hd, qt = divmod(u, 2)
                nk = META + P * (qt + 1)
                dve.wait_ge(sem("qk_done"), u + 1)
                if u >= 2:
                    dve.wait_ge(sem("prob_ready"), u - 1)
                dve.tensor_tensor_reduce(out=scb[u % 2][:, 0:nk], in0=bank[4 + u % 2][:, 0:nk],
                                         in1=cspB[:, hd, 0:nk], scale=-1.0, scalar=3.0e38, op0=ALU.add, op1=ALU.min,
                                         accum_out=nmax[:, qt, hd:hd + 1]).then_inc(sem("score_ready"), 1)
                if qt == 1 and u >= 3:
                    pt_evac(u - 3)
            pt_evac(2 * FH - 2)
            dve.wait_ge(sem("prob_ready"), 2 * FH)
            link(dve.reciprocal(rsums[:, :, :], sums[:, :, :]))
            dve.wait_ge(sem("pv_done"), 2 * FH)
            for qt in (0, 1):
                for half in (0, 1):
                    ins = dve.tensor_tensor(
                        hn[:, qt, half * 512:half * 512 + 512].rearrange("p (h e) -> p h e", e=FHD),
                        bank[2 * qt + half][:, :].rearrange("p (h e) -> p h e", e=FHD),
                        rsums[:, qt, 8 * half:8 * half + 8].unsqueeze(2).to_broadcast([P, 8, FHD]), ALU.mult)
            ins.then_inc(sem("o_ready"), 1)
            for j in range(8):
                dve.wait_ge(*done("tr", "ht1", j + 1))
                dve.tensor_copy(xT[:, j, 0:SEQ], bank[2 + j % 2][:, 0:SEQ]).then_inc(sem(f"tr_read{j % 2}"), 1)
            add_evac(1)
            moe(1)

        @block.tensor
        def _(pe):
            def project(ph, j, x, n, u_base=None):
                s = U_FIRST[ph] + j // 2
                if j % 2 == 0:
                    pe.wait_ge(arrived(s), 16 * (s // RING + 1))
                wait_bank(pe, "proj", ph, j)
                w = unit(s)
                for k in range(KB):
                    ins = pe.matmul(bank[j % 2][:, 0:n], w[:, k, (j % 2) * P:(j % 2) * P + P], x[:, k, 0:n],
                                    start=(k == 0), stop=(k == KB - 1))
                ins.then_inc(sem("proj_done"), 1)

            def norm_tr(ph, n):
                tiles = TILES if n == NT else TILES[:2]
                off = NT - n
                name = ph
                for t, _, _ in tiles:
                    pe.wait_ge(sem(f"xr_{name}"), t + 1)
                for k in range(KB):
                    wait_bank(pe, "tr", ph, k)
                    for t, rows, c0 in tiles:
                        ins = pe.transpose(bank[2 + k % 2][:, c0 - off:c0 - off + rows], xr[0:rows, t, k:D:KB],
                                           ident[0:rows, 0:rows])
                    ins.then_inc(sem("tr_done"), 1)

            def col_tr(ph, src_ph, j, tiles, off=0):
                pe.wait_ge(*read("proj", src_ph, j % 2, j // 2 + 1))
                wait_bank(pe, "tr", ph, j)
                for t, rows, c0 in tiles:
                    ins = pe.transpose(bank[2 + j % 2][0:rows, t * P:(t + 1) * P], colT[j % 2][:, c0 - off:c0 - off + rows],
                                       ident[:, :])
                ins.then_inc(sem("tr_done"), 1)

            def row_tr(ph, tiles, off=0):
                for j in range(8):
                    wait_bank(pe, "tr", ph, j)
                    for t, rows, c0 in tiles:
                        ins = pe.transpose(bank[2 + j % 2][:, c0 - off:c0 - off + rows], hn[0:rows, t, j * P:(j + 1) * P],
                                           ident[0:rows, 0:rows])
                    ins.then_inc(sem("tr_done"), 1)

            def small_mm(w, width, ready, tiles, off=0):
                for t, rows, c0 in tiles:
                    for k in range(KB):
                        ins = pe.matmul(bank[4][0:rows, t * width:(t + 1) * width],
                                        xT[:, k, c0 - off:c0 - off + rows], w[:, k, :], start=(k == 0),
                                        stop=(k == KB - 1))
                ins.then_inc(sem(ready), 1)

            pe.wait_ge(sem("ident_ready"), 1)
            norm_tr("norm0", NT)
            for b in (0, 1):
                pe.wait_ge(*read("tr", "norm0", b, 4))
            small_mm(w_gates, 8, "gate_mm", TILES)
            for j in range(4):
                project("q0", j, xT, NT)
            pe.wait_ge(sem("gate_sp"), 1)
            for b, c in ((5, 0), (6, 4)):
                for t, rows, c0 in TILES:
                    ins = pe.transpose(bank[b][0:MH, c0:c0 + rows], zg[0:rows, t, c:c + MH], ident[0:rows, 0:rows])
            ins.then_inc(sem("gate_rows"), 1)
            for j in range(4):
                project("k0", j, xT, NT)
            pe.wait_ge(sem("rows_ready"), 1)
            for t, rows, c0 in TILES:
                for a, r in ((0, row_c), (1, row_m)):
                    ins = pe.transpose(bank[4][0:rows, t * 8 + 4 * a:t * 8 + 4 * a + 4], r[:, c0:c0 + rows],
                                       ident[0:MH, 0:MH])
            ins.then_inc(sem("cm_mm"), 1)
            for hd in range(MH):
                if hd >= 2:
                    pe.wait_ge(sem("warg"), hd - 1)
                pe.matmul(bank[5 + hd % 2][:, 0:NT], negsel[:, hd, :], row_M[:, :], start=True, stop=True) \
                    .then_inc(sem("negM_mm"), 1)
            for j in range(9):
                if j < 8:
                    project("v0", j, xT, NT)
                if j >= 1:
                    col_tr("vt0", "v0", j - 1, TILES)
            for j in range(8):
                project("o0", j, xT, NT)
            for b in (0, 1):
                pe.wait_ge(*read("tr", "vt0", b, 4))
            pe.wait_ge(sem("warg"), MH)

            def head_scores(hd):
                if hd == 0:
                    pe.wait_ge(*read("proj", "q0", 1, 2))
                    pe.wait_ge(*read("proj", "k0", 1, 2))
                else:
                    pe.wait_ge(sem("st_ready"), hd)
                pe.matmul(bank[4][0:META, 0:NT], kT[:, hd, 0:META], qT[:, hd, :], start=True, stop=True)
                pe.matmul(bank[5][:, 0:SEQ], kT[:, hd, META:META + P], qT[:, hd, META:NT], start=True, stop=True)
                pe.matmul(bank[5][:, SEQ:SEQ + P], kT[:, hd, META + P:NT], qT[:, hd, META + P:NT], start=True,
                          stop=True).then_inc(sem("s_done"), 1)

            head_scores(0)
            for hd in range(MH):
                pe.wait_ge(sem("st_ready"), hd + 1)
                if hd == 0:
                    for b in (0, 1):
                        pe.wait_ge(*read("proj", "o0", b, 4))
                else:
                    pe.wait_ge(sem("num_read"), hd)
                    pe.wait_ge(sem("num_read_act"), hd)
                srcs = {2: [(0, META, 2)], 0: [(META, META, 2), (NT, P, 0)],
                        1: [(META + P, META, 2), (NT + P, P, 0), (NT + SEQ, P, 1)]}
                for t, rows, _ in TILES:
                    for n_, (c, kr, st) in enumerate(srcs[t]):
                        ins = pe.matmul(bank[t][0:rows, 0:MDV + 1], stile[0:kr, c:c + rows], v0[0:kr, st, hd, :],
                                        start=(n_ == 0), stop=(n_ == len(srcs[t]) - 1))
                ins.then_inc(sem("num_done"), 1)
                if hd + 1 < MH:
                    head_scores(hd + 1)
            pe.wait_ge(sem("num_read"), MH)
            pe.wait_ge(sem("num_read_act"), MH)
            pe.wait_ge(sem("hn_ready"), 3)
            row_tr("ht0", TILES)
            for b in (0, 1):
                pe.wait_ge(*read("tr", "ht0", b, 4))
            for j in range(9):
                if j < 8:
                    project("out0", j, xT, NT)
                if j >= 1:
                    col_tr("add0", "out0", j - 1, TILES)

            def moe(l):
                tiles = TILES[:3 - l]
                n = NT if l == 0 else SEQ
                off = NT - n
                base = U_MOE[l]
                norm_tr(f"ffn{l}", n)
                for b in (0, 1):
                    pe.wait_ge(*read("tr", f"ffn{l}", b, 4))
                if l == 0:
                    pe.wait_ge(sem("small2_loaded"), 16 * 19)
                small_mm(w_rt[:, l, :, :], NG + NE, f"router_mm{l}", tiles, off)
                pe.wait_ge(sem(f"eall_ready{l}"), 1)
                pe.wait_ge(sem("consts_ready"), 1)
                nt = len(tiles)
                jobs = [(t, rows, [(q, onesb) for q in range(t)] + [(t, upper)]) for t, rows, _ in tiles]
                for t, rows, terms in jobs + [(3, P, [(q, onesb) for q in range(nt)])]:
                    for m, (q, lhs) in enumerate(terms):
                        kr = tiles[q][1]
                        ins = pe.matmul(bank[4][0:rows, t * NE:(t + 1) * NE], lhs[0:kr, 0:rows], eall[0:kr, q, :],
                                        start=(m == 0), stop=(m == len(terms) - 1))
                ins.then_inc(sem(f"pos_mm{l}"), 1)
                pe.wait_ge(sem(f"tbl_ready{l}"), 1)

                def to_cols(b, src):
                    for j in range(4):
                        ins = pe.transpose(bank[b][:, j * P:(j + 1) * P], src[:, j:HALF:4], ident[:, :])
                    return ins

                def gate_up(b, u, x):
                    for q in range(KB):
                        j, hh = divmod(q, 2)
                        for f in (0, 1):
                            c = (4 * hh + j) * UC + f * P
                            ins = pe.matmul(bank[b][CAP * f:CAP * (f + 1), 0:2 * P], x[:, q, :],
                                            ring[:, u % RING:u % RING + 2, c:c + P], start=(q == 0), stop=(q == KB - 1))
                    return ins

                def down(b, u, a):
                    w = unit_down(u)
                    for f in (0, 1):
                        for half in (0, 1):
                            ins = pe.matmul(bank[b][CAP * half:CAP * (half + 1), :], a[:, CAP * f:CAP * (f + 1)],
                                            w[:, f, HALF * half:HALF * (half + 1)], start=(f == 0), stop=(f == 1))
                    return ins

                def overflow(i, u_gate, u_down, turns):
                    n_ = pe.value_load(tbl[0:1, bass.ds(TBL_CNT + i, 1)], min_val=0, max_val=NT)
                    op, od = sem(f"ovf_pe{l}"), sem(f"ovf_dve{l}")
                    with pe.If(n_ > CAP):
                        pe.wait_ge(arrived(u_down), turns(u_down))
                        alone(pe)
                        before_i = pe.value_load(tbl[0:1, bass.ds(TBL_OVF + i, 1)], min_val=0, max_val=NE * OVF)
                        with pe.Fori(1, OVF + 1) as tt:
                            k = before_i + tt
                            with pe.If(n_ > CAP * tt):
                                pe.wait_ge(sem(f"ox_in{l}"), 32 * k)
                                alone(pe)
                                to_cols(7, ox).then_inc(op, 1)
                                pe.wait_ge(od, 4 * k - 3)
                                alone(pe)
                                gate_up(7, u_gate, oxT).then_inc(op, 1)
                                pe.wait_ge(od, 4 * k - 2)
                                alone(pe)
                                pe.transpose(bank[7][:, 0:P], oarow, ident[:, :]).then_inc(op, 1)
                                pe.wait_ge(od, 4 * k - 1)
                                alone(pe)
                                down(7, u_down, oactT).then_inc(op, 1)
                                pe.wait_ge(od, 4 * k)
                                alone(pe)

                def act_tr(i, s, first=False):
                    pe.wait_ge(sem(f"act_ready{l}"), i)
                    if not first or s >= 3:
                        pe.wait_ge(sem(f"at_read{l}"), i - 2)
                    alone(pe)
                    pe.transpose(bank[5 + (s + 1) % 2][:, 0:P], arow[(s + 1) % 2], ident[:, :]) \
                        .then_inc(sem(f"at_done{l}"), 1)

                def turns(g, u):
                    return 16 * (g + u // RING + 1)

                def down_of(i, g, s, first=False):
                    u = expert_units(base + EU * ((s - 1) % GRP))[2]
                    pe.wait_ge(arrived(u), turns(g, u) - (16 if s == 0 else 0))
                    pe.wait_ge(sem(f"at_read{l}"), i)
                    if not first or s >= 3:
                        pe.wait_ge(sem(f"y_read{l}"), i - 2)
                    alone(pe)
                    down(3 + (s + 1) % 2, u, actT[(s + 1) % 2]).then_inc(sem(f"down_done{l}"), 1)

                def turn(i, g, s, first=False, last=False):
                    if not first or s >= 1:
                        act_tr(i, s, first)
                    pe.wait_ge(sem(f"xT_read{l}"), i + 1)
                    if not last:
                        b = (s + 1) % GRP
                        pe.wait_ge(sem(f"x_in{l}_{b}"), 16 * (g + 1 + (s + 1) // GRP))
                        alone(pe)
                        to_cols(0, xg[b]).then_inc(sem(f"tx_done{l}"), 1)
                    u_gate, u_up, u_down = expert_units(base + EU * s)
                    pe.wait_ge(arrived(u_gate), turns(g, u_gate))
                    pe.wait_ge(arrived(u_up), turns(g, u_up))
                    alone(pe)
                    gate_up(1 + s % 2, u_gate, xgT[s % 2]).then_inc(sem(f"gu_done{l}"), 1)
                    overflow(i, u_gate, u_down, lambda u: turns(g, u))
                    if not first or s >= 1:
                        down_of(i, g, s, first)

                pe.wait_ge(sem(f"x_in{l}_0"), 16)
                to_cols(0, xg[0]).then_inc(sem(f"tx_done{l}"), 1)
                for i in range(GRP):
                    turn(i, 0, i, first=True)
                with pe.Fori(1, NE // GRP - 1) as g:
                    for s in range(GRP):
                        turn(GRP * g + s, g, s)
                for i in range(NE - GRP, NE):
                    turn(i, NE // GRP - 1, i % GRP, last=i == NE - 1)
                act_tr(NE, 0)
                down_of(NE, NE // GRP, 0)
                pe.wait_ge(sem(f"y_read{l}"), NE)

            moe(0)
            norm_tr("norm1", NT)
            for b in (0, 1):
                pe.wait_ge(*read("tr", "norm1", b, 4))
            small_mm(w_f, FH, "f_mm", TILES)

            def head_norm(ph, x, n):
                for j in range(9):
                    if j < 8:
                        project(ph, j, x, n)
                    if j >= 1:
                        i = j - 1
                        pe.wait_ge(*read("proj", ph, i % 2, i // 2 + 1))
                        if i >= 2:
                            pe.wait_ge(sem(f"rstd_{ph}"), i - 1)
                        pe.matmul(bank[4 + i % 2][:, 0:n], pair_ones[:, :], sq[i % 2][:, 0:n], start=True, stop=True) \
                            .then_inc(sem(f"ssq_done_{ph}"), 1)
                    if ph == "k1" and j == 0:
                        pe.wait_ge(sem("f_sp"), 1)
                        for t, rows, c0 in TILES:
                            ins = pe.transpose(bank[6][0:FH, c0:c0 + rows], zg[0:rows, t, :], ident[0:rows, 0:rows])
                        ins.then_inc(sem("f_rows"), 1)

            head_norm("k1", xT, NT)
            for j in range(9):
                if j < 8:
                    project("v1", j, xT, NT)
                if j >= 1:
                    col_tr("vt1", "v1", j - 1, TILES)
            pe.wait_ge(sem("rstd_k1"), 8)
            head_norm("q1", xqT, SEQ)
            pe.wait_ge(sem("hn_done_q1"), 8)
            for b in (0, 1):
                pe.wait_ge(*read("tr", "vt1", b, 4))
            NU = 2 * FH

            def qk(u):
                hd, qt = divmod(u, 2)
                nk = META + P * (qt + 1)
                ph = slice(64 * (hd % 2), 64 * (hd % 2) + 64)
                if u >= 2:
                    pe.wait_ge(sem("score_ready"), u - 1)
                b = bank[4 + u % 2]
                pe.matmul(b[:, 0:nk], qT[ph, hd // 2, qt * P:(qt + 1) * P], kT[ph, hd // 2, 0:nk], start=True,
                          stop=True)
                pe.matmul(b[:, nk - P:nk], identb[:, :], mask_ts[:, :], start=False, stop=True,
                          skip_group_check=True).then_inc(sem("qk_done"), 1)

            def key_tiles(qt):
                return [(2, META, 0)] + [(t, P, META + P * t) for t in range(qt + 1)]

            def probs_tr(u):
                hd, qt = divmod(u, 2)
                pe.wait_ge(sem("prob_ready"), u + 1)
                if u >= 2:
                    pe.wait_ge(sem(f"pt_read{qt}"), hd)
                for t, rows, c0 in key_tiles(qt):
                    ins = pe.transpose(bank[6 + u % 2][0:rows, t * P:(t + 1) * P], prb[u % 2][:, c0:c0 + rows],
                                       ident[:, :])
                ins.then_inc(sem("pt_done"), 1)

            def pv(u):
                hd, qt = divmod(u, 2)
                pe.wait_ge(sem(f"pt_read{qt}"), hd + 1)
                tl = key_tiles(qt)
                o = bank[2 * qt + hd // 8][:, (hd % 8) * FHD:(hd % 8 + 1) * FHD]
                for m, (t, rows, _) in enumerate(tl):
                    ins = pe.matmul(o, ptb[u % 2][0:rows, t, :], v1[0:rows, t, hd * FHD:(hd + 1) * FHD],
                                    start=(m == 0), stop=(m == len(tl) - 1))
                ins.then_inc(sem("pv_done"), 1)

            pe.wait_ge(sem("identb_ready"), 1)
            for u in range(NU + 4):
                if u < NU:
                    qk(u)
                if 2 <= u < NU + 2:
                    probs_tr(u - 2)
                if u >= 4:
                    pv(u - 4)
            pe.wait_ge(sem("o_ready"), 1)
            row_tr("ht1", TILES[:2], META)
            for b in (0, 1):
                pe.wait_ge(*read("tr", "ht1", b, 4))
            for j in range(9):
                if j < 8:
                    project("out1", j, xT, SEQ)
                if j >= 1:
                    col_tr("add1", "out1", j - 1, TILES[:2], META)
            moe(1)


_INS = ["x", "meta_tokens", "norm_mix", "norm_ffn", "m_w_in", "m_b_gate", "m_g_out", "m_w_out", "kv_norm", "kv_w",
        "kv_b_f", "k_norm", "f_w_q", "f_q_norm", "f_w_o", "moe_w_group", "moe_b_group", "moe_w_router",
        "moe_b_router", "moe_w_gate", "moe_w_up", "moe_w_down"]


def kernel(**inputs):
    import numpy as np
    import concourse.bacc as bacc
    from concourse.bass_utils import run_bass_kernel_spmd

    nc = bacc.Bacc("TRN2", target_bir_lowering=False, num_devices=1)
    arrays, io = {}, {}
    for name in _INS:
        a = np.ascontiguousarray(inputs[name])
        arrays["in_" + name] = a
        io[name] = nc.dram_tensor("in_" + name, a.shape, mybir.dt.from_np(a.dtype), kind="ExternalInput").ap()
    out = nc.dram_tensor("out_0", (1, SEQ, D), F32, kind="ExternalOutput").ap()
    build(nc, io, out)
    r = run_bass_kernel_spmd(nc, [arrays], core_ids=[0])
    return r.results[0]["out_0"]
```
